# Optimizing a Trainium2 kernel written in Bass

```python
import jax, jax.numpy as jnp
from jax import lax
import numpy as np

D_MODEL = 1024
BATCH = 1
SEQ = 256
DEPTH = 2

GRID_W = 64
CTX_LEN = 256
N_MIXERS = 3
MOD_CHUNKS = 6
NORM_EPS = 1e-6

SGU_CHUNK = 128
SGU_WIDTH = 2 * D_MODEL
SGU_GROUPS = 8
SGU_GROUP_DIM = SGU_WIDTH // SGU_GROUPS

POOL_WINDOWS = (2, 4, 8, 16)
POOL_WIDTH = D_MODEL
POOL_GROUPS = len(POOL_WINDOWS)
POOL_GROUP_DIM = POOL_WIDTH // POOL_GROUPS

HEAD_DIM = 128
N_Q_HEADS = D_MODEL // HEAD_DIM
N_KV_HEADS = 2
Q_PER_KV = N_Q_HEADS // N_KV_HEADS
AXIS_DIM = HEAD_DIM // 2
ROPE_THETA = 10000.0
ATTN_BLOCK = 128

PEER_HEADS = 8
PEER_KEYS = 128
PEER_EXPERTS = PEER_KEYS * PEER_KEYS
PEER_TOPK = 16
PEER_QDIM = 256
PEER_HALF = PEER_QDIM // 2
PEER_CHUNK = 128

kernel_name = 'hybrid_diffusion_sgu_pool_gqa_peer'

def _rmsnorm(x, gain):
    xf = x.astype(jnp.float32)
    y = xf * lax.rsqrt(jnp.mean(xf * xf, axis=-1, keepdims=True) + NORM_EPS)
    return (y * gain.astype(jnp.float32)).astype(x.dtype)

def _modulate(x, gain, shift, scale):
    return _rmsnorm(x, gain) * (1 + scale) + shift

def _gelu(x):
    return jax.nn.gelu(x, approximate=False)

def _sgu_mixer(h, w_in, v_gain, w_s, b_s, w_out):
    bsz, length, _ = h.shape
    z = _gelu(h @ w_in)
    u, v = z[..., :SGU_WIDTH], z[..., SGU_WIDTH:]
    v = _rmsnorm(v, v_gain).reshape(bsz, length // SGU_CHUNK, SGU_CHUNK, SGU_GROUPS, SGU_GROUP_DIM)
    sv = jnp.einsum('gpq,bnqgd->bnpgd', w_s, v) + b_s.T[:, :, None]
    return (u * sv.reshape(bsz, length, SGU_WIDTH)) @ w_out

def _pool_mixer(h, w_in, w_grp, scale, w_out):
    bsz, length, _ = h.shape
    z = (h @ w_in).astype(jnp.float32).reshape(bsz, length, POOL_GROUPS, POOL_GROUP_DIM)
    cs = jnp.concatenate([jnp.zeros_like(z[:, :1]), jnp.cumsum(z, axis=1)], axis=1)
    t = jnp.arange(length)[:, None]
    half = jnp.array(POOL_WINDOWS, dtype=jnp.int32)[None, :] // 2
    lo = jnp.clip(t - half, 0, length)
    hi = jnp.clip(t + half, 0, length)
    gidx = jnp.arange(POOL_GROUPS)[None, :]
    cnt = (hi - lo).astype(jnp.float32)[None, :, :, None]
    pooled = (cs[:, hi, gidx] - cs[:, lo, gidx]) / cnt - z
    y = jnp.einsum('blgc,gcd->blgd', pooled, w_grp.astype(jnp.float32)).reshape(bsz, length, POOL_WIDTH)
    y = (y * scale.astype(jnp.float32)).astype(h.dtype)
    return y @ w_out

def _axial_rope_tables(length):
    rows = length // GRID_W
    r, col = jnp.meshgrid(jnp.arange(rows), jnp.arange(GRID_W), indexing='ij')
    pos = jnp.stack([r.reshape(-1), col.reshape(-1)], axis=-1).astype(jnp.float32)
    freqs = ROPE_THETA ** (-jnp.arange(0, AXIS_DIM, 2, dtype=jnp.float32) / AXIS_DIM)
    ang = pos[:, :, None] * freqs
    return jnp.cos(ang), jnp.sin(ang)

def _apply_axial_rope(x, cos, sin):
    xf = x.astype(jnp.float32).reshape(*x.shape[:-1], 2, AXIS_DIM)
    x1, x2 = xf[..., :AXIS_DIM // 2], xf[..., AXIS_DIM // 2:]
    c = cos[None, :, None]
    s = sin[None, :, None]
    out = jnp.concatenate([x1 * c - x2 * s, x2 * c + x1 * s], axis=-1)
    return out.reshape(x.shape).astype(x.dtype)

def _attend(q, k, v):
    s = jnp.einsum('bqhgd,bkhd->bhgqk', q, k).astype(jnp.float32) * (HEAD_DIM ** -0.5)
    p = jax.nn.softmax(s, axis=-1).astype(v.dtype)
    return jnp.einsum('bhgqk,bkhd->bqhgd', p, v)

def _attn_mixer(h_lat, h_ctx, w_qkv, q_gain, k_gain, w_o, need_ctx):
    def project(h):
        b, l, _ = h.shape
        qkv = h @ w_qkv
        nq, nk = N_Q_HEADS * HEAD_DIM, N_KV_HEADS * HEAD_DIM
        q = _rmsnorm(qkv[..., :nq].reshape(b, l, N_Q_HEADS, HEAD_DIM), q_gain)
        k = _rmsnorm(qkv[..., nq:nq + nk].reshape(b, l, N_KV_HEADS, HEAD_DIM), k_gain)
        v = qkv[..., nq + nk:].reshape(b, l, N_KV_HEADS, HEAD_DIM)
        return q, k, v

    bsz, length, _ = h_lat.shape
    ctx_len = h_ctx.shape[1]
    q_lat, k_lat, v_lat = project(h_lat)
    q_ctx, k_ctx, v_ctx = project(h_ctx)
    cos, sin = _axial_rope_tables(length)
    q_lat = _apply_axial_rope(q_lat, cos, sin).reshape(bsz, length, N_KV_HEADS, Q_PER_KV, HEAD_DIM)
    k_lat = _apply_axial_rope(k_lat, cos, sin)
    keys = jnp.concatenate([k_lat, k_ctx], axis=1)
    vals = jnp.concatenate([v_lat, v_ctx], axis=1)
    qb = q_lat.reshape(bsz, length // ATTN_BLOCK, ATTN_BLOCK, N_KV_HEADS, Q_PER_KV, HEAD_DIM).swapaxes(0, 1)
    o = lax.map(lambda blk: _attend(blk, keys, vals), qb)
    y_lat = o.swapaxes(0, 1).reshape(bsz, length, N_Q_HEADS * HEAD_DIM) @ w_o
    y_ctx = None
    if need_ctx:
        qc = q_ctx.reshape(bsz, ctx_len, N_KV_HEADS, Q_PER_KV, HEAD_DIM)
        y_ctx = _attend(qc, k_ctx, v_ctx).reshape(bsz, ctx_len, N_Q_HEADS * HEAD_DIM) @ w_o
    return y_lat, y_ctx

def _peer(h, w_q, k1, k2, u_tab, v_tab):
    n_tok = h.shape[0]
    q = (h @ w_q).reshape(n_tok, PEER_HEADS, PEER_QDIM)
    s1 = jnp.einsum('thd,hnd->thn', q[..., :PEER_HALF], k1).astype(jnp.float32)
    s2 = jnp.einsum('thd,hnd->thn', q[..., PEER_HALF:], k2).astype(jnp.float32)
    v1, i1 = lax.top_k(s1, PEER_TOPK)
    v2, i2 = lax.top_k(s2, PEER_TOPK)
    cand = (v1[..., :, None] + v2[..., None, :]).reshape(n_tok, PEER_HEADS, PEER_TOPK * PEER_TOPK)
    cidx = (i1[..., :, None] * PEER_KEYS + i2[..., None, :]).reshape(n_tok, PEER_HEADS, PEER_TOPK * PEER_TOPK)
    best, pos = lax.top_k(cand, PEER_TOPK)
    eidx = jnp.take_along_axis(cidx, pos, axis=-1)
    gate = jax.nn.softmax(best, axis=-1).astype(h.dtype)

    def block(args):
        hc, ic, gc = args
        act = jnp.einsum('chkd,cd->chk', jnp.take(u_tab, ic, axis=0), hc)
        return jnp.einsum('chk,chkd->cd', _gelu(act) * gc, jnp.take(v_tab, ic, axis=0))

    nb = n_tok // PEER_CHUNK
    out = lax.map(block, (h.reshape(nb, PEER_CHUNK, -1),
                          eidx.reshape(nb, PEER_CHUNK, PEER_HEADS, PEER_TOPK),
                          gate.reshape(nb, PEER_CHUNK, PEER_HEADS, PEER_TOPK)))
    return out.reshape(n_tok, -1)

def setup_inputs(seed: int = 0) -> dict:
    key = jax.random.key(seed)
    ks = iter(jax.random.split(key, 32))

    def nrm(shape, scale):
        return jax.random.normal(next(ks), shape, jnp.float32) * scale

    d = D_MODEL
    n_sgu = len(range(0, DEPTH, N_MIXERS))
    n_pool = len(range(1, DEPTH, N_MIXERS))
    n_attn = len(range(2, DEPTH, N_MIXERS))
    qkv_w = (N_Q_HEADS + 2 * N_KV_HEADS) * HEAD_DIM
    return {
        'x': nrm((BATCH, SEQ, d), 1.0),
        'c': nrm((BATCH, d), 1.0),
        'ctx': nrm((BATCH, CTX_LEN, d), 1.0),
        'c_ctx': nrm((d,), 1.0),
        'ada_w': nrm((DEPTH, d, MOD_CHUNKS * d), 0.5 * d ** -0.5),
        'ada_b': nrm((DEPTH, MOD_CHUNKS * d), 0.02),
        'norm1_g': 1.0 + nrm((DEPTH, d), 0.05),
        'norm2_g': 1.0 + nrm((DEPTH, d), 0.05),
        'sgu_w_in': nrm((n_sgu, d, 2 * SGU_WIDTH), d ** -0.5),
        'sgu_v_gain': 1.0 + nrm((n_sgu, SGU_WIDTH), 0.05),
        'sgu_w_s': nrm((n_sgu, SGU_GROUPS, SGU_CHUNK, SGU_CHUNK), SGU_CHUNK ** -0.5),
        'sgu_b_s': 1.0 + nrm((n_sgu, SGU_GROUPS, SGU_CHUNK), 0.05),
        'sgu_w_out': nrm((n_sgu, SGU_WIDTH, d), SGU_WIDTH ** -0.5),
        'pool_w_in': nrm((n_pool, d, POOL_WIDTH), d ** -0.5),
        'pool_w_grp': nrm((n_pool, POOL_GROUPS, POOL_GROUP_DIM, POOL_GROUP_DIM), POOL_GROUP_DIM ** -0.5),
        'pool_scale': 1.0 + nrm((n_pool, POOL_WIDTH), 0.05),
        'pool_w_out': nrm((n_pool, POOL_WIDTH, d), POOL_WIDTH ** -0.5),
        'attn_w_qkv': nrm((n_attn, d, qkv_w), d ** -0.5),
        'attn_q_gain': 1.0 + nrm((n_attn, HEAD_DIM), 0.05),
        'attn_k_gain': 1.0 + nrm((n_attn, HEAD_DIM), 0.05),
        'attn_w_o': nrm((n_attn, N_Q_HEADS * HEAD_DIM, d), (N_Q_HEADS * HEAD_DIM) ** -0.5),
        'peer_w_q': nrm((DEPTH, d, PEER_HEADS * PEER_QDIM), d ** -0.5),
        'peer_k1': nrm((DEPTH, PEER_HEADS, PEER_KEYS, PEER_HALF), PEER_HALF ** -0.5),
        'peer_k2': nrm((DEPTH, PEER_HEADS, PEER_KEYS, PEER_HALF), PEER_HALF ** -0.5),
        'peer_u': nrm((DEPTH, PEER_EXPERTS, d), d ** -0.5),
        'peer_v': nrm((DEPTH, PEER_EXPERTS, d), PEER_HEADS ** -0.5),
        'final_gain': 1.0 + nrm((d,), 0.05),
    }

def reference(x, c, ctx, c_ctx, ada_w, ada_b, norm1_g, norm2_g, sgu_w_in, sgu_v_gain, sgu_w_s, sgu_b_s,
              sgu_w_out, pool_w_in, pool_w_grp, pool_scale, pool_w_out, attn_w_qkv, attn_q_gain, attn_k_gain,
              attn_w_o, peer_w_q, peer_k1, peer_k2, peer_u, peer_v, final_gain):
    bsz, seq, d = x.shape
    ctx_len = ctx.shape[1]
    x_lat, x_ctx = x, ctx
    for i in range(DEPTH):
        kind, j = i % N_MIXERS, i // N_MIXERS
        need_ctx = i < DEPTH - 1
        mod_lat = jnp.split((jax.nn.silu(c) @ ada_w[i] + ada_b[i])[:, None, :], MOD_CHUNKS, axis=-1)
        mod_ctx = jnp.split((jax.nn.silu(c_ctx) @ ada_w[i] + ada_b[i])[None, None, :], MOD_CHUNKS, axis=-1)

        h_lat = _modulate(x_lat, norm1_g[i], mod_lat[0], mod_lat[1])
        h_ctx = _modulate(x_ctx, norm1_g[i], mod_ctx[0], mod_ctx[1]) if (need_ctx or kind == 2) else None
        y_ctx = None
        if kind == 0:
            y_lat = _sgu_mixer(h_lat, sgu_w_in[j], sgu_v_gain[j], sgu_w_s[j], sgu_b_s[j], sgu_w_out[j])
            if need_ctx:
                y_ctx = _sgu_mixer(h_ctx, sgu_w_in[j], sgu_v_gain[j], sgu_w_s[j], sgu_b_s[j], sgu_w_out[j])
        elif kind == 1:
            y_lat = _pool_mixer(h_lat, pool_w_in[j], pool_w_grp[j], pool_scale[j], pool_w_out[j])
            if need_ctx:
                y_ctx = _pool_mixer(h_ctx, pool_w_in[j], pool_w_grp[j], pool_scale[j], pool_w_out[j])
        else:
            y_lat, y_ctx = _attn_mixer(h_lat, h_ctx, attn_w_qkv[j], attn_q_gain[j], attn_k_gain[j],
                                       attn_w_o[j], need_ctx)
        x_lat = x_lat + mod_lat[2] * y_lat
        if need_ctx:
            x_ctx = x_ctx + mod_ctx[2] * y_ctx

        f_lat_in = _modulate(x_lat, norm2_g[i], mod_lat[3], mod_lat[4]).reshape(bsz * seq, d)
        if need_ctx:
            f_ctx_in = _modulate(x_ctx, norm2_g[i], mod_ctx[3], mod_ctx[4]).reshape(bsz * ctx_len, d)
            f = _peer(jnp.concatenate([f_lat_in, f_ctx_in], axis=0), peer_w_q[i], peer_k1[i], peer_k2[i],
                      peer_u[i], peer_v[i])
            f_lat = f[:bsz * seq]
            x_ctx = x_ctx + mod_ctx[5] * f[bsz * seq:].reshape(bsz, ctx_len, d)
        else:
            f_lat = _peer(f_lat_in, peer_w_q[i], peer_k1[i], peer_k2[i], peer_u[i], peer_v[i])
        x_lat = x_lat + mod_lat[5] * f_lat.reshape(bsz, seq, d)
    return _rmsnorm(x_lat, final_gain)


_drawn_inputs = setup_inputs


def setup_inputs(seed=0):
    import zlib

    import numpy as np

    out = dict(_drawn_inputs(seed))
    spreads = {}
    factors = {'norm2_g': 2.966, 'sgu_v_gain': 4.01, 'sgu_b_s': 4.168, 'pool_scale': 4.04}
    for name, (base, spread) in spreads.items():
        noise = np.random.default_rng([zlib.crc32(name.encode()), seed]).standard_normal(out[name].shape)
        drawn = base * np.exp(spread * noise) if base else spread * noise
        out[name] = __import__('jax').numpy.asarray(drawn.astype(out[name].dtype))
    for name, factor in factors.items():
        out[name] = (out[name] * factor).astype(out[name].dtype)
    return out
```

```python
from contextlib import ExitStack

import concourse.bass as bass
import numpy as np
from concourse import mybir

P = 128
D = 1024
KT = D // P
T = 256
TT = T // P
LAYERS = 2
CHUNKS = 6
EPS = 1e-6
SGU_W = 2048
SGU_FT = SGU_W // P
SGU_G = 8
HEADS = 8
KEYS = 128
TOPK = 16
HK = HEADS * TOPK
PG = 4
PAD = 8
EXP_TILES = KEYS
RAW = 4
BANKS = 4
HALF = 512
GRP = 4
NGRP = T // GRP

STREAM = [("w_in", 0, 32), ("w_out", 0, 16), ("w_q", 0, 16), ("u", 0, EXP_TILES), ("v", 0, EXP_TILES),
          ("p_in", 1, 8), ("p_out", 1, 8), ("w_q", 1, 16), ("u", 1, EXP_TILES), ("v", 1, EXP_TILES)]
BASE = {}
TOTAL = 0
for _name, _layer, _tiles in STREAM:
    BASE[_name, _layer] = TOTAL
    TOTAL += _tiles


def build(nc, xt_d, c_d, ada_d, adab_d, n1_d, n2_d, fg_d, w_in_d, vg_d, ws_d, bs_d, w_out_d, p_in_d, p_grp_d,
          ps_d, p_out_d, w_q_d, k1_d, k2_d, u_d, v_d, out_d):
    fp32, f32r, u32 = mybir.dt.float32, mybir.dt.float32r, mybir.dt.uint32
    ALU, ACT, AX = mybir.AluOpType, mybir.ActivationFunctionType, mybir.AxisListType
    ds = bass.ds

    stream_dram = {("w_in", 0): w_in_d, ("w_out", 0): w_out_d, ("p_in", 1): p_in_d, ("p_out", 1): p_out_d}
    for layer in range(LAYERS):
        stream_dram["w_q", layer] = w_q_d[layer]
        stream_dram["u", layer] = u_d[layer]
        stream_dram["v", layer] = v_d[layer]

    ctx = ExitStack()
    with ctx:
        def sb(name, shape, dt=fp32, at=None):
            return (at or ctx).enter_context(nc.sbuf_tensor(name, shape, dt))

        def sem(name):
            return ctx.enter_context(nc.semaphore(name))

        XT = sb("XT", [P, KT, T])
        hH = sb("hH", [P, KT, T], f32r)
        hL = sb("hL", [P, KT, T], f32r)
        raw = [sb(f"raw{s}", [P, KT * P]) for s in range(RAW)]
        wH = [sb(f"wH{s}", [P, HALF], f32r) for s in range(4)]
        wL = [sb(f"wL{s}", [P, HALF], f32r) for s in range(4)]
        gateH = [sb(f"gateH{s}", [P, T], f32r) for s in range(2)]
        gateL = [sb(f"gateL{s}", [P, T], f32r) for s in range(2)]
        mod = sb("mod", [P, LAYERS * CHUNKS * KT])
        adab = sb("adab", [P, LAYERS * CHUNKS * KT])
        n1 = sb("n1", [P, LAYERS * KT])
        n2 = sb("n2", [P, LAYERS * KT])
        fg = sb("fg", [P, KT])
        vg = sb("vg", [P, SGU_FT])
        ps = sb("ps", [P, KT])
        csT = sb("csT", [P, KT])
        gs = sb("gs", [P, 5, KT])
        eps = sb("eps", [P, 1])
        mean_w = sb("mean_w", [P, P])
        ident = sb("ident", [P, P])
        iota = sb("iota", [P, KEYS])
        iota_k = sb("iota_k", [P, TOPK])
        rstd = sb("rstd", [P, T])
        std = sb("std", [P, T])
        tick = sb("tick", [P, 4])
        ssq = sb("ssq", [P, 2])
        sel = sb("sel", [P, 3, TT, HK])
        selT = sb("selT", [P, 3, T])

        oneA = [sb(f"oneA{s}", [P, GRP, KEYS]) for s in range(2)]
        oneB = [sb(f"oneB{s}", [P, GRP, KEYS]) for s in range(2)]

        with ExitStack() as mix:
            UV = sb("UV", [P, 32, T], at=mix)
            vtok = sb("vtok", [P, TT, SGU_W], at=mix)
            gH = sb("gH", [P, SGU_FT, T], f32r, at=mix)
            gL = sb("gL", [P, SGU_FT, T], f32r, at=mix)
            sq = sb("sq", [P, KT, T], at=mix)
            hf = sb("hf", [P, KT, T], at=mix)
            bs = sb("bs", [P, SGU_G, P], at=mix)
            ws = sb("ws", [P, SGU_G, P], at=mix)
            keys = sb("keys", [P, 2, HEADS, KEYS], at=mix)
            Z = sb("Z", [P, KT, PAD + T + PAD], at=mix)
        with ExitStack() as tk:
            sb("under_topk", [P, 80 * T], at=tk)
            S = sb("S", [P, TT, 2 * HEADS, KEYS], at=tk)
            C = sb("C", [P, HEADS, TOPK * TOPK], at=tk)
            M = sb("M", [P, HK // 2, TOPK], at=tk)
            top_v = sb("top_v", [P, TT, 2 * HEADS, TOPK], at=tk)
            top_i = sb("top_i", [P, TT, 2 * HEADS, TOPK], u32, at=tk)
            top_f = sb("top_f", [P, TT, 2 * HEADS, TOPK], at=tk)
            best = sb("best", [P, TT, HEADS, TOPK], at=tk)
            pos = sb("pos", [P, TT, HEADS, TOPK], u32, at=tk)
            pos_ab = sb("pos_ab", [P, 2, TT, HK], u32, at=tk)
            ab = sb("ab", [P, 2, TT, HK], at=tk)
            ex = sb("ex", [P, TT, HEADS, TOPK], at=tk)
            zsum = sb("zsum", [P, TT * HEADS], at=tk)
        with ExitStack() as rr:
            R = sb("R", [P, EXP_TILES, T], at=rr)
        with ExitStack() as oo:
            otok = sb("otok", [P, TT, D], at=oo)

        ring = [ctx.enter_context(nc.psum_tensor(f"ring{b}", [P, 512], fp32)) for b in range(BANKS)]
        O = [ctx.enter_context(nc.psum_tensor(f"O{b}", [P, 512], fp32)) for b in range(4)]

        s_small = sem("s_small")
        s_const = sem("s_const")
        s_silu = sem("s_silu")
        s_ada = [sem(f"s_ada{s}") for s in range(8)]
        s_ada_used = sem("s_ada_used")
        s_mod = sem("s_mod")
        s_raw = [sem(f"s_raw{s}") for s in range(RAW)]
        s_h = sem("s_h")
        s_l = sem("s_l")
        s_pe = sem("s_pe")
        s_bank_a = sem("s_bank_a")
        s_bank_v = sem("s_bank_v")
        s_sq = sem("s_sq")
        s_ms = sem("s_ms")
        s_std = sem("s_std")
        s_hf = sem("s_hf")
        s_hH = sem("s_hH")
        s_hin = sem("s_hin")
        s_x = sem("s_x")
        s_vt = sem("s_vt")
        s_vc = sem("s_vc")
        s_ssq = sem("s_ssq")
        s_vn = sem("s_vn")
        s_mixed = sem("s_mixed")
        s_sv = sem("s_sv")
        s_gf = sem("s_gf")
        s_gH = sem("s_gH")
        s_gL = sem("s_gL")
        s_sc = sem("s_sc")
        s_scc = sem("s_scc")
        s_diff = sem("s_diff")
        s_exp = sem("s_exp")
        s_sel = sem("s_sel")
        s_selT = sem("s_selT")
        s_selc = sem("s_selc")
        s_one = sem("s_one")
        s_grid = sem("s_grid")
        s_gated = sem("s_gated")
        s_gH2 = sem("s_gH2")
        s_gL2 = sem("s_gL2")
        s_oc = sem("s_oc")
        s_ot = sem("s_ot")
        s_pg = sem("s_pg")
        s_pooled = sem("s_pooled")
        s_late = sem("s_late")
        s_vstep = sem("s_vstep")
        s_out = sem("s_out")

        block = ctx.enter_context(nc.Block())

        def modcol(layer, chunk, j=0, n=KT):
            at = (layer * CHUNKS + chunk) * KT + j
            return mod[:, at:at + n]

        small_loads = [(XT[:, :, :], xt_d), (csT[:, :], c_d), (adab[:, :], adab_d), (n1[:, :], n1_d),
                       (n2[:, :], n2_d), (fg[:, :], fg_d), (vg[:, :], vg_d), (ps[:, :], ps_d),
                       (bs[:, :, :], bs_d), (ws[:, :, :], ws_d), (keys[:, 0], k1_d[0]), (keys[:, 1], k2_d[0])]
        SMALL = 16 * len(small_loads)
        NORMS = 2 * LAYERS + 1
        ADA_TILES = LAYERS * CHUNKS * KT

        @block.sync
        def _(sp):
            for dst, src in small_loads:
                sp.dma_start(dst, src).then_inc(s_small, 16)
            for s in range(8):
                sp.dma_start(UV[:, 4 * s:4 * s + 4, :], ada_d[s]).then_inc(s_ada[s], 16)
            with sp.Fori(1, ADA_TILES // 8) as i:
                for s in range(8):
                    sp.wait_ge(s_ada_used, 8 * i + (s - 7))
                    sp.dma_start(UV[:, 4 * s:4 * s + 4, :], ada_d[ds(8 * i + s, 1)]).then_inc(s_ada[s], 16)
            for name, layer, tiles in STREAM:
                src = stream_dram[name, layer]
                base = BASE[name, layer]
                first = 0
                if base == 0:
                    for s in range(RAW):
                        sp.dma_start(raw[s][:, :], src[s]).then_inc(s_raw[s], 16)
                    first = 1
                with sp.Fori(first, tiles // RAW) as i:
                    for s in range(RAW):
                        sp.wait_ge(s_l, 8 * i + (2 * (base + s) - 6))
                        sp.dma_start(raw[s][:, :], src[ds(4 * i + s, 1)]).then_inc(s_raw[s], 16)
            sp.wait_ge(s_hf, NORMS)
            sp.dma_start(out_d, hf[:, :, :]).then_inc(s_out, 16)
            sp.wait_ge(s_out, 16)

        @block.gpsimd
        def _(pool):
            pool.memset(ident[:, :], 0.0).then_inc(s_const, 1)
            pool.memset(mean_w[:, :], 1.0 / D).then_inc(s_const, 1)
            pool.memset(eps[:, :], EPS).then_inc(s_const, 1)
            pool.iota(iota[:, :], [[1, KEYS]], base=0, channel_multiplier=0,
                      allow_small_or_imprecise_dtypes=True).then_inc(s_const, 1)
            pool.iota(iota_k[:, :], [[1, TOPK]], base=0, channel_multiplier=0,
                      allow_small_or_imprecise_dtypes=True).then_inc(s_const, 1)
            pool.wait_ge(s_const, 5)
            pool.affine_select(out=ident[:, :], in_=ident[:, :], compare_op=ALU.not_equal, fill=1.0, base=0,
                               pattern=[[-1, P]], channel_multiplier=1).then_inc(s_const, 1)
            pool.wait_ge(s_x, 2)
            pool.dma_start(keys[:, 0], k1_d[1]).then_inc(s_late, 16)
            pool.dma_start(keys[:, 1], k2_d[1]).then_inc(s_late, 16)
            pool.dma_start(UV[:, 0:8, :], p_grp_d).then_inc(s_late, 16)

        @block.scalar
        def _(act):
            def split_high(base, i, s, steps=(0, 1)):
                for half in steps:
                    q = 8 * i + (2 * (base + s) + half)
                    if half == 0:
                        act.wait_ge(s_raw[s % RAW], 16 * i + (base + s) // 4 * 16 + 16)
                    if not (isinstance(q, int) and q < 4):
                        act.wait_ge(s_pe, q - 3)
                    nc.scalar.activation(wH[(2 * s + half) % 4][:, :], raw[s % RAW][:, half * HALF:half * HALF + HALF],
                                         ACT.Copy).then_inc(s_h, 1)

            def ahead(base, i, s, end=False):
                if not end:
                    split_high(base, i, s + 2)

            def norm(n):
                act.wait_ge(s_x, n) if n else act.wait_ge(s_small, SMALL)
                nc.scalar.activation(sq[:, :, :], XT[:, :, :], ACT.Square).then_inc(s_sq, 1)
                act.wait_ge(s_ms, n + 1)
                nc.scalar.activation(std[:, :], O[0][:, 0:T], ACT.Sqrt, bias=eps[:, :]).then_inc(s_std, 1)
                if n < NORMS - 1:
                    act.wait_ge(s_hf, n + 1)
                    nc.scalar.activation(hH[:, :, :], hf[:, :, :], ACT.Copy).then_inc(s_hH, 1)

            act.wait_ge(s_small, SMALL)
            act.wait_ge(s_const, 6)
            nc.scalar.activation(csT[:, :], csT[:, :], ACT.Silu).then_inc(s_silu, 1)
            split_high(0, 0, 0)
            split_high(0, 0, 1)
            norm(0)
            for layer in range(LAYERS):
                if layer == 0:
                    with act.Fori(0, 32 // 4) as i:
                        for s in range(4):
                            ahead(BASE["w_in", 0], i, s)
                            nc.scalar.activation(UV[:, ds(4 * i + s, 1), :], ring[s][:, 0:T], ACT.Gelu)\
                                .then_inc(s_bank_a, 1)
                    for blk in range(8):
                        c, f = blk // 4, blk % 4
                        act.wait_ge(s_vt, blk + 1)
                        src = ring[blk] if blk < 4 else O[blk - 4]
                        nc.scalar.activation(vtok[:, c, f * 512:f * 512 + 512], src[:, :], ACT.Copy).then_inc(s_vc, 1)
                    for c in range(TT):
                        act.wait_ge(s_vc, 4 * c + 4)
                        nc.scalar.activation(sq[:, :, :].rearrange("p a b -> p (a b)"), vtok[:, c, :], ACT.Square,
                                             accum_out=ssq[:, c:c + 1]).then_inc(s_ssq, 1)
                        act.wait_ge(s_ssq, c + 1)
                    nc.scalar.activation(std[:, 0:2], ssq[:, :], ACT.Sqrt, bias=eps[:, :], scale=1.0 / SGU_W)\
                        .then_inc(s_ssq, 1)
                    for f in range(SGU_FT):
                        act.wait_ge(s_gf, f + 1)
                        nc.scalar.activation(gH[:, f, :], UV[:, SGU_FT + f, :], ACT.Copy).then_inc(s_gH, 1)
                    with act.Fori(0, 16 // 4) as i:
                        for s in range(4):
                            ahead(BASE["w_out", 0], i, s)
                else:
                    with act.Fori(0, 8 // 4) as i:
                        for s in range(4):
                            ahead(BASE["p_in", 1], i, s)
                    for f in range(KT):
                        act.wait_ge(s_gf, SGU_FT + f + 1)
                        nc.scalar.activation(gH[:, f, :], UV[:, 24 + f, :], ACT.Copy).then_inc(s_gH, 1)
                    with act.Fori(0, 8 // 4) as i:
                        for s in range(4):
                            ahead(BASE["p_out", 1], i, s)
                norm(2 * layer + 1)
                with act.Fori(0, 16 // 4) as i:
                    for s in range(4):
                        ahead(BASE["w_q", layer], i, s)
                        nc.scalar.activation(UV[:, ds(4 * i + s, 1), :], ring[s][:, 0:T], ACT.Copy)\
                            .then_inc(s_bank_a, 1)
                def experts(lo, hi):
                    with act.Fori(lo // 4, hi // 4) as i:
                        for s in range(4):
                            ahead(BASE["u", layer], i, s)
                            nc.scalar.activation(R[:, ds(4 * i + s, 1), :], ring[s][:, 0:T], ACT.Gelu)\
                                .then_inc(s_bank_a, 1)
                experts(0, 64)
                act.wait_ge(s_diff, layer + 1)
                nc.scalar.activation(best[:, :, :, :], ex[:, :, :, :], ACT.Exp).then_inc(s_exp, 1)
                experts(64, 80)
                act.wait_ge(s_sel, layer + 1)
                experts(80, 128)
                act.wait_ge(s_gated, 4 + (layer + 1) * NGRP)

                def split_gated(i, s):
                    nc.scalar.activation(gateH[s % 2][:, :], R[:, ds(4 * i + s, 1), :].rearrange("p a t -> p (a t)"),
                                         ACT.Copy).then_inc(s_gH2, 1)

                split_gated(0, 0)
                with act.Fori(0, 31) as i:
                    for s in range(4):
                        split_gated(i, s + 1)
                        ahead(BASE["v", layer], i, s)
                for s in range(4):
                    if s < 3:
                        split_gated(31, s + 1)
                    ahead(BASE["v", layer], 31, s, end=(layer == LAYERS - 1 and s >= 2))
                act.wait_ge(s_pe, 2 * (BASE["v", layer] + 128))
                for b in range(2):
                    nc.scalar.activation(otok[:, 0, 512 * b:512 * b + 512], O[b][:, :], ACT.Copy).then_inc(s_oc, 1)
                norm(2 * layer + 2)

        @block.vector
        def _(dve):
            steps = [0]

            def step(ins):
                steps[0] += 1
                ins.then_inc(s_vstep, 1)
                return steps[0]

            def after(n):
                dve.wait_ge(s_vstep, n)

            def split_low(base, i, s):
                for half in range(2):
                    dve.wait_ge(s_h, 8 * i + (2 * (base + s) + half + 1))
                    nc.vector.tensor_tensor(wL[(2 * s + half) % 4][:, :],
                                            raw[s % RAW][:, half * HALF:half * HALF + HALF],
                                            wH[(2 * s + half) % 4][:, :].bitcast(fp32), ALU.subtract).then_inc(s_l, 1)

            def ahead(base, i, s, end=False):
                if not end:
                    split_low(base, i, s + 2)

            def norm(n):
                dve.wait_ge(s_std, n + 1)
                after(step(nc.vector.reciprocal(rstd[:, :], std[:, :])))
                after(step(nc.vector.tensor_tensor(sq[:, :, :], XT[:, :, :],
                                                   rstd[:, None, :].to_broadcast([P, KT, T]), ALU.mult)))
                for k in range(KT):
                    if n == NORMS - 1:
                        last = nc.vector.tensor_scalar(hf[:, k, :], sq[:, k, :], fg[:, k:k + 1], None, ALU.mult)
                    else:
                        last = nc.vector.tensor_scalar(hf[:, k, :], sq[:, k, :], gs[:, n, k:k + 1],
                                                       modcol(n // 2, 3 * (n % 2), k, 1), ALU.mult, ALU.add)
                last.then_inc(s_hf, 1)
                if n < NORMS - 1:
                    dve.wait_ge(s_hH, n + 1)
                    nc.vector.tensor_tensor(hL[:, :, :], hf[:, :, :], hH[:, :, :].bitcast(fp32), ALU.subtract)\
                        .then_inc(s_hin, 1)

            def residual(layer, chunk, j, bank, half):
                return nc.vector.scalar_tensor_tensor(XT[:, j, :], bank[:, half * T:half * T + T],
                                                      modcol(layer, chunk, j, 1), XT[:, j, :], ALU.mult, ALU.add)

            nc.vector.memset(tick[:, 1:2], 0.0).then_inc(s_bank_v, 4)
            nc.vector.memset(tick[:, 2:3], 0.0).then_inc(s_bank_a, 4)
            nc.vector.memset(tick[:, 3:4], 0.0).then_inc(s_gated, 4)
            split_low(0, 0, 0)
            split_low(0, 0, 1)
            dve.wait_ge(s_small, SMALL)
            dve.wait_ge(s_ada_used, ADA_TILES)
            after(step(nc.vector.tensor_tensor(mod[:, :], O[1][:, 0:ADA_TILES], adab[:, :], ALU.add)))
            for layer in range(LAYERS):
                for m, gain in ((0, n1), (1, n2)):
                    n = 2 * layer + m
                    last = step(nc.vector.scalar_tensor_tensor(gs[:, n, :], modcol(layer, 3 * m + 1), 1.0,
                                                               gain[:, layer * KT:layer * KT + KT], ALU.add, ALU.mult))
            after(last)

            norm(0)
            for layer in range(LAYERS):
                if layer == 0:
                    with dve.Fori(0, 32 // 4) as i:
                        for s in range(4):
                            ahead(BASE["w_in", 0], i, s)
                    dve.wait_ge(s_ssq, 3)
                    after(step(nc.vector.reciprocal(rstd[:, 0:2], std[:, 0:2])))
                    for c in range(TT):
                        last = nc.vector.tensor_scalar(vtok[:, c, :], vtok[:, c, :], rstd[:, c:c + 1], None, ALU.mult)
                        last.then_inc(s_vn, 1)
                    for f in range(SGU_FT):
                        dve.wait_ge(s_mixed, f + 1)
                        g = f // (SGU_FT // SGU_G)
                        view = hf[:, f % 8, :].rearrange("p (c t) -> p c t", c=TT)
                        nc.vector.scalar_tensor_tensor(
                            view, ring[f % 4][:, 0:T].rearrange("p (c t) -> p c t", c=TT), vg[:, f:f + 1],
                            bs[:, g:g + 1, :].to_broadcast([P, TT, P]), ALU.mult, ALU.add).then_inc(s_sv, 1)
                        dve.wait_ge(s_sv, f + 1)
                        nc.vector.tensor_tensor(UV[:, SGU_FT + f, :], hf[:, f % 8, :], UV[:, f, :], ALU.mult)\
                            .then_inc(s_gf, 1)
                        if f:
                            dve.wait_ge(s_gH, f)
                            nc.vector.tensor_tensor(gL[:, f - 1, :], UV[:, SGU_FT + f - 1, :],
                                                    gH[:, f - 1, :].bitcast(fp32), ALU.subtract).then_inc(s_gL, 1)
                    dve.wait_ge(s_gH, SGU_FT)
                    nc.vector.tensor_tensor(gL[:, SGU_FT - 1, :], UV[:, 2 * SGU_FT - 1, :],
                                            gH[:, SGU_FT - 1, :].bitcast(fp32), ALU.subtract).then_inc(s_gL, 1)
                    base = BASE["w_out", 0]
                    for j in range(KT):
                        for s in range(2):
                            ahead(base, j // 2, 2 * (j % 2) + s)
                        dve.wait_ge(s_pe, 2 * (base + 2 * j + 2))
                        residual(0, 2, j, ring[j % 4], 0).then_inc(s_bank_v, 1)
                    dve.wait_ge(s_bank_v, 4 + 8)
                    nc.vector.memset(tick[:, 0:1], 0.0).then_inc(s_x, 1)
                else:
                    place = UV[:, 12, :]
                    hi_t, lo_t = UV[:, 13, :], UV[:, 14, :]
                    dve.wait_ge(s_const, 6)
                    last = step(nc.vector.tensor_scalar(UV[:, 12, 0:P], iota[:, :], 0.0, None, ALU.add))
                    last = step(nc.vector.tensor_scalar(UV[:, 12, P:T], iota[:, :], float(P), None, ALU.add))
                    last = step(nc.vector.memset(Z[:, :, 0:PAD], 0.0))
                    last = step(nc.vector.memset(Z[:, :, PAD + T:], 0.0))
                    after(last)
                    for g in range(PG):
                        half = float(1 << g)
                        last = step(nc.vector.tensor_scalar(hi_t, place, half, float(T), ALU.add, ALU.min))
                        last = step(nc.vector.tensor_scalar(lo_t, place, -half, 0.0, ALU.add, ALU.max))
                        after(last)
                        after(step(nc.vector.tensor_tensor(hi_t, hi_t, lo_t, ALU.subtract)))
                        after(step(nc.vector.reciprocal(UV[:, 8 + g, :], hi_t)))
                    base = BASE["p_in", 1]
                    for j in range(KT):
                        ahead(base, j // 4, j % 4)
                        dve.wait_ge(s_pe, 2 * (base + j + 1))
                        nc.vector.tensor_copy(Z[:, j, PAD:PAD + T], ring[j % 4][:, 0:T]).then_inc(s_bank_v, 1)
                    dve.wait_ge(s_bank_v, 4 + 16)
                    W = PAD + T + PAD
                    lev = [sq[:, :, :].rearrange("p a b -> p (a b)")[:, a * 2 * W:(a + 1) * 2 * W]
                           .rearrange("p (c w) -> p c w", c=2) for a in range(2)]
                    for g in range(PG):
                        z2 = Z[:, 2 * g:2 * g + 2, :]
                        after(step(nc.vector.tensor_tensor(lev[0][:, :, 1:W - 1], z2[:, :, 0:W - 2], z2[:, :, 1:W - 1],
                                                           ALU.add)))
                        lo, hi, cur = 1, W - 1, 0
                        for m in range(1, g + 1):
                            r = 1 << (m - 1)
                            lo, hi = lo + r, hi - r
                            after(step(nc.vector.tensor_tensor(lev[1 - cur][:, :, lo:hi], lev[cur][:, :, lo - r:hi - r],
                                                               lev[cur][:, :, lo + r:hi + r], ALU.add)))
                            cur = 1 - cur
                        pooled = vtok[:, 0, 2 * g * T:(2 * g + 2) * T].rearrange("p (c t) -> p c t", c=2)
                        after(step(nc.vector.tensor_tensor(pooled, lev[cur][:, :, PAD:PAD + T],
                                                           UV[:, 8 + g:9 + g, :].to_broadcast([P, 2, T]), ALU.mult)))
                        nc.vector.tensor_tensor(pooled, pooled, z2[:, :, PAD:PAD + T], ALU.subtract).then_inc(s_pooled, 1)
                    for f in range(KT):
                        dve.wait_ge(s_pg, f + 1)
                        src = (ring[f] if f < 4 else O[f - 4])[:, 0:T]
                        nc.vector.tensor_scalar(UV[:, 24 + f, :], src, ps[:, f:f + 1], None, ALU.mult).then_inc(s_gf, 1)
                        if f:
                            dve.wait_ge(s_gH, SGU_FT + f)
                            nc.vector.tensor_tensor(gL[:, f - 1, :], UV[:, 23 + f, :], gH[:, f - 1, :].bitcast(fp32),
                                                    ALU.subtract).then_inc(s_gL, 1)
                    dve.wait_ge(s_gH, SGU_FT + KT)
                    nc.vector.tensor_tensor(gL[:, KT - 1, :], UV[:, 31, :], gH[:, KT - 1, :].bitcast(fp32),
                                            ALU.subtract).then_inc(s_gL, 1)
                    base = BASE["p_out", 1]
                    for j in range(KT):
                        ahead(base, j // 4, j % 4)
                        dve.wait_ge(s_pe, 2 * (base + j + 1))
                        residual(1, 2, j, ring[j % 4], 0).then_inc(s_bank_v, 1)
                    dve.wait_ge(s_bank_v, 4 + 24)
                    nc.vector.memset(tick[:, 0:1], 0.0).then_inc(s_x, 1)
                norm(2 * layer + 1)
                with dve.Fori(0, 16 // 4) as i:
                    for s in range(4):
                        ahead(BASE["w_q", layer], i, s)
                for b in range(8):
                    dve.wait_ge(s_sc, 8 * layer + b + 1)
                    nc.vector.tensor_copy(S[:, b // 4, 4 * (b % 4):4 * (b % 4) + 4, :],
                                          (ring[b] if b < 4 else O[b - 4])[:, :].rearrange("p (a n) -> p a n", a=4))\
                        .then_inc(s_scc, 1)
                dve.wait_ge(s_scc, 8 * layer + 8)

                def top16(values, out_v, out_i):
                    after(step(nc.vector.max(out_v[:, 0:8], values)))
                    a = step(nc.vector.max_index(out_i[:, 0:8], out_v[:, 0:8], values))
                    after(a)
                    after(step(nc.vector.match_replace(values, out_v[:, 0:8], values, -3.0e38)))
                    after(step(nc.vector.max(out_v[:, 8:16], values)))
                    return step(nc.vector.max_index(out_i[:, 8:16], out_v[:, 8:16], values))

                def topk_step(n):
                    if n < 32:
                        tt, j = n // 16, n % 16
                        top16(S[:, tt, j, :], top_v[:, tt, j, :], top_i[:, tt, j, :])
                    elif n < 48:
                        tt, h = (n - 32) // 8, (n - 32) % 8
                        if h == 0:
                            after(steps[0])
                            v = top_v[:, tt, :, :].rearrange("p (h s) k -> p h s k", s=2)
                            after(step(nc.vector.tensor_tensor(
                                C[:, :, :].rearrange("p h (a b) -> p h a b", a=TOPK),
                                v[:, :, 0, :, None].to_broadcast([P, HEADS, TOPK, TOPK]),
                                v[:, :, 1, None, :].to_broadcast([P, HEADS, TOPK, TOPK]), ALU.add)))
                        top16(C[:, h, :], best[:, tt, h, :], pos[:, tt, h, :])
                    elif n == 48:
                        after(steps[0])
                        flat = pos[:, :, :, :].rearrange("p t h k -> p t (h k)")
                        step(nc.vector.tensor_scalar(pos_ab[:, 0], flat, 4, None, ALU.logical_shift_right))
                        step(nc.vector.tensor_scalar(pos_ab[:, 1], flat, 15, None, ALU.bitwise_and))
                        nc.vector.tensor_tensor(
                            ex[:, :, :, :].rearrange("p t h k -> p (t h) k"), best[:, :, :, :].rearrange("p t h k -> p (t h) k"),
                            best[:, :, :, 0:1].rearrange("p t h k -> p (t h) k").to_broadcast([P, TT * HEADS, TOPK]),
                            ALU.subtract).then_inc(s_diff, 1)
                        after(steps[0])
                    elif n == 49:
                        step(nc.vector.tensor_copy(ab[:, :, :, :], pos_ab[:, :, :, :]))
                        step(nc.vector.tensor_copy(top_f[:, :, :, :], top_i[:, :, :, :]))
                        after(steps[0])
                    elif n < 74:
                        tt, side, hh, what = (n - 50) // 12, (n - 50) // 6 % 2, (n - 50) // 3 % 2, (n - 50) % 3
                        half = HK // 2
                        if what == 0:
                            after(step(nc.vector.tensor_tensor(
                                M[:, :, :], ab[:, side, tt, hh * half:hh * half + half, None].to_broadcast([P, half, TOPK]),
                                iota_k[:, None, :].to_broadcast([P, half, TOPK]), ALU.is_equal)))
                        elif what == 1:
                            keys_of = top_f[:, tt, :, :].rearrange("p (h s) k -> p h s k", s=2)[:, 4 * hh:4 * hh + 4, side, None, :]
                            m4 = M[:, :, :].rearrange("p (h k) a -> p h k a", h=4)
                            after(step(nc.vector.tensor_tensor(m4, m4, keys_of.to_broadcast([P, 4, TOPK, TOPK]), ALU.mult)))
                        else:
                            after(step(nc.vector.tensor_reduce(sel[:, side, tt, hh * half:hh * half + half], M[:, :, :],
                                                               AX.X, ALU.add)))
                    elif n == 74:
                        dve.wait_ge(s_exp, layer + 1)
                        after(step(nc.vector.tensor_reduce(zsum[:, :], best[:, :, :, :].rearrange("p t h k -> p (t h) k"),
                                                           AX.X, ALU.add)))
                        after(step(nc.vector.reciprocal(zsum[:, :], zsum[:, :])))
                        nc.vector.tensor_tensor(
                            sel[:, 2, :, :].rearrange("p t (h k) -> p (t h) k", h=HEADS),
                            best[:, :, :, :].rearrange("p t h k -> p (t h) k"),
                            zsum[:, :, None].to_broadcast([P, TT * HEADS, TOPK]), ALU.mult).then_inc(s_sel, 1)

                base = BASE["u", layer]
                for n in range(76):
                    ahead(base, n // 4, n % 4)
                    topk_step(n)
                with dve.Fori(76 // 4, 128 // 4) as i:
                    for s in range(4):
                        ahead(base, i, s)

                dve.wait_ge(s_selT, layer + 1)
                for a in range(3):
                    step(nc.vector.tensor_copy(selT[:, a, :], O[a][:, 0:T]))
                after(steps[0])

                def one_hots(i, s):
                    for t in range(GRP):
                        tok = GRP * (4 * i + s) + t
                        nc.vector.tensor_scalar(oneA[s % 2][:, t, :], iota[:, :], selT[:, 0, ds(tok, 1)],
                                                selT[:, 2, ds(tok, 1)], ALU.is_equal, ALU.mult)
                        last = nc.vector.tensor_scalar(oneB[s % 2][:, t, :], iota[:, :], selT[:, 1, ds(tok, 1)], None,
                                                       ALU.is_equal)
                    last.then_inc(s_one, 1)

                def gate(i, s):
                    dve.wait_ge(s_grid, 4 * i + (layer * NGRP + s + 1))
                    r = R[:, :, ds(GRP * (4 * i + s), GRP)]
                    nc.vector.tensor_tensor(r, ring[s][:, :].rearrange("p (t n) -> p n t", t=GRP), r, ALU.mult)\
                        .then_inc(s_gated, 1)

                dve.wait_ge(s_bank_a, 4 + 32 + 144 * (layer + 1))
                with dve.Fori(0, NGRP // 4) as i:
                    for s in (0, 2):
                        one_hots(i, s)
                        one_hots(i, s + 1)
                        gate(i, s)
                        gate(i, s + 1)
                dve.wait_ge(s_gated, 4 + (layer + 1) * NGRP)

                def split_gated(i, s):
                    dve.wait_ge(s_gH2, 4 * i + (layer * EXP_TILES + s + 1))
                    nc.vector.tensor_tensor(gateL[s % 2][:, :], R[:, ds(4 * i + s, 1), :].rearrange("p a t -> p (a t)"),
                                            gateH[s % 2][:, :].bitcast(fp32), ALU.subtract).then_inc(s_gL2, 1)

                base = BASE["v", layer]
                split_gated(0, 0)
                with dve.Fori(0, 31) as i:
                    for s in range(4):
                        split_gated(i, s + 1)
                        ahead(base, i, s)
                for s in range(4):
                    if s < 3:
                        split_gated(31, s + 1)
                    ahead(base, 31, s, end=(layer == LAYERS - 1 and s >= 2))
                dve.wait_ge(s_pe, 2 * (base + 128))
                for b in range(2):
                    nc.vector.tensor_copy(otok[:, 1, 512 * b:512 * b + 512], O[2 + b][:, :]).then_inc(s_oc, 1)
                for j in range(KT):
                    if j % 2 == 0:
                        dve.wait_ge(s_ot, layer * 4 + j // 2 + 1)
                    step(residual(layer, 5, j, ring[j // 2], j % 2))
                after(steps[0])
                nc.vector.memset(tick[:, 0:1], 0.0).then_inc(s_x, 1)
                norm(2 * layer + 2)

        @block.tensor
        def _(pe):
            mm = nc.tensor.matmul

            def tile_product(base, i, s, bank, xH, xL, k0=0, first=True, last=True):
                for half in range(2):
                    pe.wait_ge(s_l, 8 * i + (2 * (base + s) + half + 1))
                    slot = (2 * s + half) % 4
                    for kk in range(4):
                        k = 4 * half + kk
                        a, b = wH[slot][:, kk * P:kk * P + P], wL[slot][:, kk * P:kk * P + P]
                        mm(bank[:, 0:T], a, xH[:, k0 + k, :], start=(first and k == 0), stop=False)
                        mm(bank[:, 0:T], a, xL[:, k0 + k, :], start=False, stop=False)
                        ins = mm(bank[:, 0:T], b, xH[:, k0 + k, :], start=False, stop=(last and k == KT - 1))
                    ins.then_inc(s_pe, 1)

            def stage(name, layer, emptied, before):
                base = BASE[name, layer]
                tiles = {"w_in": 32, "w_q": 16, "u": EXP_TILES, "p_in": 8, "p_out": 8}[name]
                xH, xL = (gH, gL) if name == "p_out" else (hH, hL)
                with pe.Fori(0, tiles // 4) as i:
                    for s in range(4):
                        pe.wait_ge(emptied, 4 * i + (before + s + 1))
                        tile_product(base, i, s, ring[s], xH, xL)

            def norm(n):
                pe.wait_ge(s_sq, n + 1)
                for k in range(KT):
                    ins = mm(O[0][:, 0:T], mean_w[:, :], sq[:, k, :], start=(k == 0), stop=(k == KT - 1))
                ins.then_inc(s_ms, 1)

            pe.wait_ge(s_silu, 1)
            pe.wait_ge(s_const, 6)
            with pe.Fori(0, ADA_TILES // 8) as i:
                for s in range(8):
                    pe.wait_ge(s_ada[s], 16 * i + 16)
                    w = UV[:, 4 * s:4 * s + 4, :].rearrange("p a b -> p (a b)")
                    for k in range(KT):
                        ins = mm(O[1][:, ds(8 * i + s, 1)], w[:, k * P:k * P + P], csT[:, k:k + 1],
                                 start=(k == 0), stop=(k == KT - 1))
                    ins.then_inc(s_ada_used, 1)

            norm(0)
            for layer in range(LAYERS):
                pe.wait_ge(s_hin, 2 * layer + 1)
                if layer == 0:
                    stage("w_in", 0, s_bank_a, 0)
                    pe.wait_ge(s_bank_a, 4 + 32)
                    for blk in range(8):
                        c, f = blk // 4, blk % 4
                        dst = ring[blk] if blk < 4 else O[blk - 4]
                        for q in range(4):
                            ins = nc.tensor.transpose(dst[:, q * P:q * P + P], UV[:, SGU_FT + 4 * f + q, c * P:c * P + P],
                                                      ident[:, :])
                        ins.then_inc(s_vt, 1)
                    pe.wait_ge(s_vn, TT)
                    for f in range(SGU_FT):
                        if f >= 4:
                            pe.wait_ge(s_sv, f - 3)
                        for c in range(TT):
                            ins = mm(ring[f % 4][:, c * P:c * P + P], vtok[:, c, f * P:f * P + P],
                                     ws[:, f // (SGU_FT // SGU_G), :], start=True, stop=True)
                        ins.then_inc(s_mixed, 1)
                    pe.wait_ge(s_gL, SGU_FT)
                    for j in range(KT):
                        pe.wait_ge(s_bank_v, j + 1)
                        for kk in range(2):
                            tile_product(BASE["w_out", 0], j // 2, 2 * (j % 2) + kk, ring[j % 4], gH, gL, KT * kk,
                                         first=(kk == 0), last=(kk == 1))
                else:
                    stage("p_in", 1, s_bank_v, 8)
                    pe.wait_ge(s_late, 48)
                    for f in range(KT):
                        g = f // 2
                        pe.wait_ge(s_pooled, g + 1)
                        dst = ring[f] if f < 4 else O[f - 4]
                        wg = UV[:, 0:8, :].rearrange("p a b -> p (a b)")
                        for kk in range(2):
                            at = (2 * f + kk) * P
                            ins = mm(dst[:, 0:T], wg[:, at:at + P],
                                     vtok[:, 0, (2 * g + kk) * T:(2 * g + kk + 1) * T], start=(kk == 0), stop=(kk == 1))
                        ins.then_inc(s_pg, 1)
                    pe.wait_ge(s_gL, SGU_FT + KT)
                    stage("p_out", 1, s_bank_v, 16)
                norm(2 * layer + 1)
                pe.wait_ge(s_hin, 2 * layer + 2)
                stage("w_q", layer, s_bank_a, 32 + 144 * layer)
                pe.wait_ge(s_bank_a, 4 + 48 + 144 * layer)
                for b in range(8):
                    tt, j0 = b // 4, 4 * (b % 4)
                    dst = ring[b] if b < 4 else O[b - 4]
                    for j in range(j0, j0 + 4):
                        ins = mm(dst[:, (j - j0) * P:(j - j0 + 1) * P], UV[:, j, tt * P:tt * P + P],
                                 keys[:, j % 2, j // 2, :], start=True, stop=True)
                    ins.then_inc(s_sc, 1)
                pe.wait_ge(s_scc, 8 * layer + 8)
                stage("u", layer, s_bank_a, 48 + 144 * layer)
                pe.wait_ge(s_sel, layer + 1)
                for a in range(3):
                    for tt in range(TT):
                        ins = nc.tensor.transpose(O[a][:, tt * P:tt * P + P], sel[:, a, tt, :], ident[:, :])
                ins.then_inc(s_selT, 1)
                pe.wait_ge(s_bank_a, 4 + 32 + 144 * (layer + 1))
                with pe.Fori(0, NGRP // 4) as i:
                    for s in range(4):
                        pe.wait_ge(s_one, 4 * i + (layer * NGRP + s + 1))
                        pe.wait_ge(s_gated, 4 * i + (layer * NGRP + s + 1))
                        for t in range(GRP):
                            ins = mm(ring[s][:, t * KEYS:(t + 1) * KEYS], oneB[s % 2][:, t, :], oneA[s % 2][:, t, :],
                                     start=True, stop=True)
                        ins.then_inc(s_grid, 1)

                base = BASE["v", layer]

                def values(i, s, first=False, last=False):
                    pe.wait_ge(s_gL2, 4 * i + (layer * EXP_TILES + s + 1))
                    for half in range(2):
                        pe.wait_ge(s_l, 8 * i + (2 * (base + s) + half + 1))
                        slot = (2 * s + half) % 4
                        for tt in range(TT):
                            o = O[2 * tt + half]
                            a = gateH[s % 2][:, tt * P:tt * P + P]
                            b = gateL[s % 2][:, tt * P:tt * P + P]
                            mm(o[:, :], a, wH[slot][:, :], start=first, stop=False)
                            mm(o[:, :], a, wL[slot][:, :], start=False, stop=False)
                            ins = mm(o[:, :], b, wH[slot][:, :], start=False, stop=last)
                        ins.then_inc(s_pe, 1)

                for s in range(4):
                    values(0, s, first=(s == 0))
                with pe.Fori(1, 31) as i:
                    for s in range(4):
                        values(i, s)
                for s in range(4):
                    values(31, s, last=(s == 3))
                pe.wait_ge(s_oc, 4 * (layer + 1))
                for j in range(KT):
                    for tt in range(TT):
                        ins = nc.tensor.transpose(ring[j // 2][:, (j % 2) * T + tt * P:(j % 2) * T + tt * P + P],
                                                  otok[:, tt, j * P:j * P + P], ident[:, :])
                    if j % 2:
                        ins.then_inc(s_ot, 1)
                norm(2 * layer + 2)


def tiles_of(w, n_in):
    n = w.shape[-1]
    w = w.reshape(n_in, KT, P, n // P, P).transpose(3, 0, 2, 1, 4)
    return np.ascontiguousarray(w.reshape(n // P * n_in, P, KT * P))


def kernel(**inputs):
    import concourse.bacc as bacc
    from concourse.bass_utils import run_bass_kernel_spmd

    a = {k: np.asarray(v) for k, v in inputs.items()}

    def cols(w):
        return np.ascontiguousarray(w.reshape(-1, P).T)

    arrays = {
        "xt": np.ascontiguousarray(a["x"][0].reshape(T, KT, P).transpose(2, 1, 0)),
        "c": cols(a["c"]),
        "ada": np.concatenate([tiles_of(a["ada_w"][i], 1) for i in range(LAYERS)]),
        "adab": cols(a["ada_b"]),
        "n1": cols(a["norm1_g"]),
        "n2": cols(a["norm2_g"]),
        "fg": cols(a["final_gain"]),
        "w_in": tiles_of(a["sgu_w_in"][0], 1),
        "vg": cols(a["sgu_v_gain"]),
        "ws": np.ascontiguousarray(a["sgu_w_s"][0].transpose(2, 0, 1)),
        "bs": np.ascontiguousarray(np.broadcast_to(a["sgu_b_s"][0], (P, SGU_G, P))),
        "w_out": tiles_of(a["sgu_w_out"][0], 2),
        "p_in": tiles_of(a["pool_w_in"][0], 1),
        "p_grp": np.ascontiguousarray(
            a["pool_w_grp"][0].reshape(PG, 2, P, 2, P).transpose(2, 0, 3, 1, 4).reshape(P, 8, T)),
        "ps": cols(a["pool_scale"]),
        "p_out": tiles_of(a["pool_w_out"][0], 1),
        "w_q": np.stack([tiles_of(a["peer_w_q"][i], 1) for i in range(LAYERS)]),
        "k1": np.ascontiguousarray(a["peer_k1"].transpose(0, 3, 1, 2)),
        "k2": np.ascontiguousarray(a["peer_k2"].transpose(0, 3, 1, 2)),
        "u": np.ascontiguousarray(a["peer_u"].reshape(LAYERS, EXP_TILES, P, KT, P).transpose(0, 1, 4, 3, 2)
                                  .reshape(LAYERS, EXP_TILES, P, KT * P)),
        "v": a["peer_v"].reshape(LAYERS, EXP_TILES, P, D),
    }
    nc = bacc.Bacc("TRN2", target_bir_lowering=False, num_devices=1)
    args = [nc.dram_tensor(f"in_{k}", v.shape, mybir.dt.from_np(v.dtype), kind="ExternalInput").ap()
            for k, v in arrays.items()]
    out = nc.dram_tensor("out_t", (P, KT, T), mybir.dt.float32, kind="ExternalOutput").ap()
    build(nc, *args, out)
    r = run_bass_kernel_spmd(nc, [{f"in_{k}": v for k, v in arrays.items()}], core_ids=[0])
    return r.results[0]["out_t"].transpose(2, 1, 0).reshape(1, T, D)
```

```python
from contextlib import ExitStack

import concourse.bass as bass
import numpy as np
from concourse import mybir

P = 128
D = 1024
KT = D // P
T = 256
TT = T // P
LAYERS = 2
CHUNKS = 6
EPS = 1e-6
SGU_W = 2048
SGU_FT = SGU_W // P
SGU_G = 8
HEADS = 8
KEYS = 128
TOPK = 16
HK = HEADS * TOPK
PG = 4
PAD = 8
EXP_TILES = KEYS
RAW = 4
BANKS = 4
HALF = 512
ADA_AT = 32
GRP = 4
NGRP = T // GRP

POOL_ORDER = [6, 7, 4, 5, 2, 3, 0, 1]

STREAM = [("w_v", 0, 16), ("w_u", 0, 16), ("w_out", 0, 16), ("w_q", 0, 16), ("u", 0, EXP_TILES), ("v", 0, EXP_TILES),
          ("p_in", 1, 8), ("p_out", 1, 8), ("w_q", 1, 16), ("u", 1, EXP_TILES), ("v", 1, EXP_TILES)]
BASE = {}
TOTAL = 0
for _name, _layer, _tiles in STREAM:
    BASE[_name, _layer] = TOTAL
    TOTAL += _tiles


def build(nc, xt_d, c_d, ada_d, adab_d, n1_d, n2_d, fg_d, w_in_d, vg_d, ws_d, bs_d, w_out_d, p_in_d, p_grp_d,
          ps_d, p_out_d, w_q_d, k1_d, k2_d, u_d, v_d, out_d):
    fp32, f32r, u32 = mybir.dt.float32, mybir.dt.float32r, mybir.dt.uint32
    ALU, ACT, AX = mybir.AluOpType, mybir.ActivationFunctionType, mybir.AxisListType
    ds = bass.ds

    stream_dram = {("w_v", 0): w_in_d[SGU_FT:2 * SGU_FT], ("w_u", 0): w_in_d[0:SGU_FT], ("w_out", 0): w_out_d, ("p_in", 1): p_in_d, ("p_out", 1): p_out_d}
    for layer in range(LAYERS):
        stream_dram["w_q", layer] = w_q_d[layer]
        stream_dram["u", layer] = u_d[layer]
        stream_dram["v", layer] = v_d[layer]

    ctx = ExitStack()
    with ctx:
        def sb(name, shape, dt=fp32, at=None):
            return (at or ctx).enter_context(nc.sbuf_tensor(name, shape, dt))

        def sem(name):
            return ctx.enter_context(nc.semaphore(name))

        XT = sb("XT", [P, KT, T])
        raw = [sb(f"raw{s}", [P, KT * P]) for s in range(RAW)]
        wH = [sb(f"wH{s}", [P, HALF], f32r) for s in range(4)]
        wL = [sb(f"wL{s}", [P, HALF], f32r) for s in range(4)]
        with ExitStack() as one:
            hH = sb("hH", [P, KT, T], f32r, at=one)
            hL = sb("hL", [P, KT, T], f32r, at=one)
            gateH = [sb(f"gateH{x}", [P, T], f32r, at=one) for x in range(2)]
            gateL = [sb(f"gateL{x}", [P, T], f32r, at=one) for x in range(2)]
        oneA = [sb(f"oneA{x}", [P, GRP, KEYS]) for x in range(4)]
        oneB = [sb(f"oneB{x}", [P, GRP, KEYS]) for x in range(4)]
        dist = [sb(f"dist{x}", [P, GRP, KEYS]) for x in range(2)]
        mod = sb("mod", [P, LAYERS * CHUNKS * KT])
        adab = sb("adab", [P, LAYERS * CHUNKS * KT])
        n1 = sb("n1", [P, LAYERS * KT])
        n2 = sb("n2", [P, LAYERS * KT])
        fg = sb("fg", [P, KT])
        vg = sb("vg", [P, SGU_FT])
        ps = sb("ps", [P, KT])
        csT = sb("csT", [P, KT])
        gs = sb("gs", [P, 5, KT])
        eps = sb("eps", [P, 1])
        mean_w = sb("mean_w", [P, P])
        ident = sb("ident", [P, P])
        iota = sb("iota", [P, KEYS])
        iota_k = sb("iota_k", [P, TOPK])
        rstd = sb("rstd", [P, T])
        std = sb("std", [P, T])
        tick = sb("tick", [P, 8])
        ssq = sb("ssq", [P, 8])
        ssum = sb("ssum", [P, TT])
        vstd = sb("vstd", [P, TT])
        ones = sb("ones", [P, 1])
        picks = sb("picks", [P, 3, 4 * GRP])
        picks_a = sb("picks_a", [P, 4 * GRP])
        sel = sb("sel", [P, 3, TT, HK])
        selT = sb("selT", [P, 3, T])

        with ExitStack() as mix:
            UV = sb("UV", [P, 32, T], at=mix)
            gH = sb("gH", [P, SGU_FT, T], f32r, at=mix)
            gL = sb("gL", [P, SGU_FT, T], f32r, at=mix)
            vtok = sb("vtok", [P, TT, SGU_W], at=mix)
            sq = sb("sq", [P, KT, T], at=mix)
            hf = sb("hf", [P, KT, T], at=mix)
            bs = sb("bs", [P, SGU_G, P], at=mix)
            ws = sb("ws", [P, SGU_G, P], at=mix)
            keys = sb("keys", [P, 2, HEADS, KEYS], at=mix)
            Z = sb("Z", [P, KT, PAD + T + PAD], at=mix)
        with ExitStack() as ad:
            sb("under_ada", [P, ADA_AT * T], at=ad)
            ada = [sb(f"ada{x}", [P, D], at=ad) for x in range(4)]
            acc = sb("acc", [P, 7, D], at=ad)
        with ExitStack() as tk:
            sb("under_topk", [P, 80 * T], at=tk)
            S = sb("S", [P, TT, 2 * HEADS, KEYS], at=tk)
            C = sb("C", [P, HEADS, TOPK * TOPK], at=tk)
            M = sb("M", [P, HK // 2, TOPK], at=tk)
            top_v = sb("top_v", [P, TT, 2 * HEADS, TOPK], at=tk)
            top_i = sb("top_i", [P, TT, 2 * HEADS, TOPK], u32, at=tk)
            top_f = sb("top_f", [P, TT, 2 * HEADS, TOPK], at=tk)
            best = sb("best", [P, TT, HEADS, TOPK], at=tk)
            pos = sb("pos", [P, TT, HEADS, TOPK], u32, at=tk)
            pos_ab = sb("pos_ab", [P, 2, TT, HK], u32, at=tk)
            ab = sb("ab", [P, 2, TT, HK], at=tk)
            ex = sb("ex", [P, TT, HEADS, TOPK], at=tk)
            zsum = sb("zsum", [P, TT * HEADS], at=tk)
        with ExitStack() as rr:
            R = sb("R", [P, EXP_TILES, T], at=rr)
        with ExitStack() as oo:
            otok = sb("otok", [P, TT, D], at=oo)

        ring = [ctx.enter_context(nc.psum_tensor(f"ring{b}", [P, 512], fp32)) for b in range(BANKS)]
        O = [ctx.enter_context(nc.psum_tensor(f"O{b}", [P, 512], fp32)) for b in range(4)]

        s_first = sem("s_first")
        s_small = sem("s_small")
        s_const = sem("s_const")
        s_silu = sem("s_silu")
        s_ada = [sem(f"s_ada{x}") for x in range(4)]
        s_acc = sem("s_acc")
        s_modp = sem("s_modp")
        s_mod = sem("s_mod")
        s_raw = [sem(f"s_raw{x}") for x in range(RAW)]
        s_h = sem("s_h")
        s_l0 = sem("s_l0")
        s_l1 = sem("s_l1")
        s_pe = sem("s_pe")
        s_bank_a = sem("s_bank_a")
        s_bank_v = sem("s_bank_v")
        s_res = sem("s_res")
        s_sq = sem("s_sq")
        s_ms = sem("s_ms")
        s_std = sem("s_std")
        s_xn = sem("s_xn")
        s_hf = sem("s_hf")
        s_hH = sem("s_hH")
        s_hin = sem("s_hin")
        s_vt = sem("s_vt")
        s_vc = sem("s_vc")
        s_ssq = sem("s_ssq")
        s_vstd = sem("s_vstd")
        s_vn = sem("s_vn")
        s_mixed = sem("s_mixed")
        s_sv = sem("s_sv")
        s_gf = sem("s_gf")
        s_gH = sem("s_gH")
        s_gL = sem("s_gL")
        s_sc = sem("s_sc")
        s_scc = sem("s_scc")
        s_diff = sem("s_diff")
        s_exp = sem("s_exp")
        s_sel = sem("s_sel")
        s_selT = sem("s_selT")
        s_selc = sem("s_selc")
        s_pick = sem("s_pick")
        s_pick_a = sem("s_pick_a")
        s_dist = sem("s_dist")
        s_oneA = sem("s_oneA")
        s_oneB = sem("s_oneB")
        s_grid = sem("s_grid")
        s_gated = sem("s_gated")
        s_gH2 = sem("s_gH2")
        s_gL2 = sem("s_gL2")
        s_oc = sem("s_oc")
        s_ot = sem("s_ot")
        s_pooled = sem("s_pooled")
        s_pg = sem("s_pg")
        s_late = sem("s_late")
        s_vstep = sem("s_vstep")
        s_out = sem("s_out")

        block = ctx.enter_context(nc.Block())

        def pool_bank(n):
            return O[n % 4]

        def score_bank(b, tt):
            return O[2 * (b % 2) + tt]

        def modcol(layer, chunk, j=0, n=KT):
            at = (layer * CHUNKS + chunk) * KT + j
            return mod[:, at:at + n]

        small_loads = [(csT[:, :], c_d), (adab[:, :], adab_d), (n1[:, :], n1_d), (XT[:, :, :], xt_d),
                       (n2[:, :], n2_d), (fg[:, :], fg_d), (vg[:, :], vg_d), (ps[:, :], ps_d),
                       (bs[:, :, :], bs_d), (ws[:, :, :], ws_d), (keys[:, 0], k1_d[0]), (keys[:, 1], k2_d[0])]
        FIRST = 4
        SMALL = 16 * (len(small_loads) - FIRST)
        NORMS = 2 * LAYERS + 1
        ADA_FRONT, ADA_MLP, ADA_V = 2 * KT, 3 * KT, 7 * KT
        ADA_FROM = EXP_TILES - ADA_V
        W_V, W_U, W_OUT = BASE["w_v", 0], BASE["w_u", 0], BASE["w_out", 0]
        ACT_EVACS = 32
        ACT_PER_LAYER = 16 + EXP_TILES

        @block.sync
        def _(sp):
            def load(src, base, i, s, first=False):
                if not first:
                    sp.wait_ge(s_l0, 4 * i + (base + s - 3))
                    sp.wait_ge(s_l1, 4 * i + (base + s - 3))
                tile = src[s] if first else src[ds(4 * i + s, 1)]
                sp.dma_start(raw[s][:, :], tile).then_inc(s_raw[s], 16)

            def load_ada(m, s, first=False):
                if not first:
                    sp.wait_ge(s_acc, m - 3)
                sp.dma_start(ada[s][:, :], ada_d[m] if isinstance(m, int) else ada_d[ds(m, 1)]).then_inc(s_ada[s], 16)

            for dst, src in small_loads[:FIRST]:
                sp.dma_start(dst, src).then_inc(s_first, 16)
            for s in range(4):
                load_ada(s, s, first=True)
            with sp.Fori(1, ADA_FRONT // 4) as i:
                for s in range(4):
                    load_ada(4 * i + s, s)
            for s in range(RAW):
                load(stream_dram["w_v", 0], 0, 0, s, first=True)
            for dst, src in small_loads[FIRST:]:
                sp.dma_start(dst, src).then_inc(s_small, 16)
            for s in range(4):
                load_ada(ADA_FRONT + s, s)
            with sp.Fori(1, 16 // 4) as i:
                for s in range(4):
                    load(stream_dram["w_v", 0], 0, i, s)
                    load_ada(4 * i + (ADA_FRONT + s), s)
            with sp.Fori(0, (ADA_MLP - 16) // 4) as i:
                for s in range(4):
                    load(stream_dram["w_u", 0], W_U, i, s)
                    load_ada(4 * i + (ADA_FRONT + 16 + s), s)
            with sp.Fori((ADA_MLP - 16) // 4, 16 // 4) as i:
                for s in range(4):
                    load(stream_dram["w_u", 0], W_U, i, s)
            for name, layer, tiles in STREAM[2:]:
                src, base = stream_dram[name, layer], BASE[name, layer]
                beside_ada = (name, layer) == ("v", 0)
                with sp.Fori(0, (ADA_FROM if beside_ada else tiles) // 4) as i:
                    for s in range(4):
                        load(src, base, i, s)
                if beside_ada:
                    with sp.Fori(ADA_FROM // 4, EXP_TILES // 4) as i:
                        for s in range(4):
                            load(src, base, i, s)
                            load_ada(4 * i + (ADA_FRONT + ADA_MLP - ADA_FROM + s), s)
            for p in range(4):
                sp.wait_ge(s_hf, 4 * (NORMS - 1) + p + 1)
                sp.dma_start(out_d[:, 2 * p:2 * p + 2, :], hf[:, 2 * p:2 * p + 2, :]).then_inc(s_out, 16)
            sp.wait_ge(s_out, 64)

        @block.gpsimd
        def _(pool):
            pool.memset(ident[:, :], 0.0).then_inc(s_const, 1)
            pool.memset(mean_w[:, :], 1.0 / D).then_inc(s_const, 1)
            pool.memset(eps[:, :], EPS).then_inc(s_const, 1)
            pool.memset(ones[:, :], 1.0).then_inc(s_const, 1)
            pool.iota(iota[:, :], [[1, KEYS]], base=0, channel_multiplier=0,
                      allow_small_or_imprecise_dtypes=True).then_inc(s_const, 1)
            pool.iota(iota_k[:, :], [[1, TOPK]], base=0, channel_multiplier=0,
                      allow_small_or_imprecise_dtypes=True).then_inc(s_const, 1)
            pool.wait_ge(s_const, 6)
            pool.affine_select(out=ident[:, :], in_=ident[:, :], compare_op=ALU.not_equal, fill=1.0, base=0,
                               pattern=[[-1, P]], channel_multiplier=1).then_inc(s_const, 1)

            def low_second(g, s):
                pool.wait_ge(s_h, 2 * g + 2)
                nc.gpsimd.tensor_tensor(wL[(2 * s + 1) % 4][:, :], raw[s][:, HALF:2 * HALF],
                                        wH[(2 * s + 1) % 4][:, :].bitcast(fp32), ALU.subtract).then_inc(s_l1, 1)

            with pool.Fori(0, BASE["p_in", 1] // 4) as i:
                for s in range(4):
                    low_second(4 * i + s, s)
            pool.wait_ge(s_res, KT)
            pool.dma_start(keys[:, 0], k1_d[1]).then_inc(s_late, 16)
            pool.dma_start(keys[:, 1], k2_d[1]).then_inc(s_late, 16)
            pool.dma_start(UV[:, 0:8, :], p_grp_d).then_inc(s_late, 16)
            with pool.Fori(BASE["p_in", 1] // 4, TOTAL // 4) as i:
                for s in range(4):
                    low_second(4 * i + s, s)

        @block.scalar
        def _(act):
            def split_high(base, i, s):
                for half in range(2):
                    q = 8 * i + (2 * (base + s) + half)
                    if half == 0:
                        act.wait_ge(s_raw[s % RAW], 16 * i + (base + s) // 4 * 16 + 16)
                    if not (isinstance(q, int) and q < 4):
                        act.wait_ge(s_pe, q - 3)
                    nc.scalar.activation(wH[(2 * s + half) % 4][:, :], raw[s % RAW][:, half * HALF:half * HALF + HALF],
                                         ACT.Copy).then_inc(s_h, 1)

            def ahead(base, i, s):
                split_high(base, i, s + 2)

            def square(j):
                return nc.scalar.activation(sq[:, j, :], XT[:, j, :], ACT.Square).then_inc(s_sq, 1)

            def norm(n):
                act.wait_ge(s_ms, n + 1)
                nc.scalar.activation(std[:, :], O[0][:, 0:T], ACT.Sqrt, bias=eps[:, :]).then_inc(s_std, 1)
                for p in range(4):
                    act.wait_ge(s_xn, 4 * n + p + 1)
                    for k in (2 * p, 2 * p + 1):
                        if n == NORMS - 1:
                            ins = nc.scalar.activation(hf[:, k, :], sq[:, k, :], ACT.Copy, scale=fg[:, k:k + 1])
                        else:
                            ins = nc.scalar.activation(hf[:, k, :], sq[:, k, :], ACT.Identity,
                                                       bias=modcol(n // 2, 3 * (n % 2), k, 1), scale=gs[:, n, k:k + 1])
                    ins.then_inc(s_hf, 1)
                    if n < NORMS - 1:
                        act.wait_ge(s_hf, 4 * n + p + 1)
                        nc.scalar.activation(hH[:, 2 * p:2 * p + 2, :], hf[:, 2 * p:2 * p + 2, :], ACT.Copy)\
                            .then_inc(s_hH, 1)

            def gated_high(f, count):
                act.wait_ge(s_gf, count)
                nc.scalar.activation(gH[:, f, :], UV[:, SGU_FT + f, :], ACT.Copy).then_inc(s_gH, 1)

            act.wait_ge(s_first, 16 * FIRST)
            nc.scalar.activation(csT[:, :], csT[:, :], ACT.Silu).then_inc(s_silu, 1)
            for j in range(KT):
                square(j)
            split_high(0, 0, 0)
            split_high(0, 0, 1)
            act.wait_ge(s_const, 7)
            act.wait_ge(s_mod, 1)
            norm(0)
            act.wait_ge(s_small, SMALL)
            for layer in range(LAYERS):
                if layer == 0:
                    with act.Fori(0, 16 // 4) as i:
                        for s in range(4):
                            ahead(W_V, i, s)
                            nc.scalar.activation(UV[:, ds(4 * i + (SGU_FT + s), 1), :], ring[s][:, 0:T], ACT.Gelu)\
                                .then_inc(s_bank_a, 1)
                    for t in range(16):
                        ahead(W_U, t // 4, t % 4)
                        nc.scalar.activation(UV[:, t, :], ring[t % 4][:, 0:T], ACT.Gelu).then_inc(s_bank_a, 1)
                        if t < 8:
                            c, f = t // 4, t % 4
                            act.wait_ge(s_vt, t + 1)
                            nc.scalar.activation(vtok[:, c, f * 512:f * 512 + 512], O[f][:, :], ACT.Copy)
                            nc.scalar.activation((sq, hf)[c][:, 2 * f:2 * f + 2, :].rearrange("p a b -> p (a b)"), O[f][:, :], ACT.Square,
                                                 accum_out=ssq[:, t:t + 1]).then_inc(s_vc, 1)
                        if t == 8:
                            act.wait_ge(s_ssq, 1)
                            nc.scalar.activation(vstd[:, :], ssum[:, :], ACT.Sqrt, bias=eps[:, :], scale=1.0 / SGU_W)\
                                .then_inc(s_vstd, 1)
                        if t > 10:
                            for f in (2 * (t - 11), 2 * (t - 11) + 1):
                                gated_high(f, f + 1)
                    for f in range(10, SGU_FT):
                        gated_high(f, f + 1)
                    for j in range(KT):
                        for kk in range(2):
                            ahead(W_OUT, j // 2, 2 * (j % 2) + kk)
                        if j:
                            act.wait_ge(s_bank_v, 4 + j)
                            square(j - 1)
                    act.wait_ge(s_bank_v, 4 + KT)
                    square(KT - 1)
                else:
                    base = BASE["p_in", 1]
                    for j in range(KT):
                        ahead(base, j // 4, j % 4)
                    for f in range(KT):
                        gated_high(POOL_ORDER[f], SGU_FT + f + 1)
                    base = BASE["p_out", 1]
                    for j in range(KT):
                        ahead(base, j // 4, j % 4)
                        if j:
                            act.wait_ge(s_bank_v, 4 + 16 + j)
                            square(j - 1)
                    act.wait_ge(s_bank_v, 4 + 16 + KT)
                    square(KT - 1)
                norm(2 * layer + 1)
                with act.Fori(0, 16 // 4) as i:
                    for s in range(4):
                        ahead(BASE["w_q", layer], i, s)
                        nc.scalar.activation(UV[:, ds(4 * i + s, 1), :], ring[s][:, 0:T], ACT.Copy)\
                            .then_inc(s_bank_a, 1)

                def experts(lo, hi):
                    with act.Fori(lo // 4, hi // 4) as i:
                        for s in range(4):
                            ahead(BASE["u", layer], i, s)
                            nc.scalar.activation(R[:, ds(4 * i + s, 1), :], ring[s][:, 0:T], ACT.Gelu)\
                                .then_inc(s_bank_a, 1)

                experts(0, 60)
                act.wait_ge(s_diff, layer + 1)
                nc.scalar.activation(best[:, :, :, :], ex[:, :, :, :], ACT.Exp).then_inc(s_exp, 1)
                experts(60, 80)
                act.wait_ge(s_sel, layer + 1)
                experts(80, 128)

                act.wait_ge(s_selc, 3 * (layer + 1))
                with act.Fori(0, NGRP // 4) as i:
                    nc.scalar.activation(picks_a[:, :], selT[:, 1, ds(4 * GRP * i, 4 * GRP)], ACT.Copy)\
                        .then_inc(s_pick_a, 1)
                    act.wait_ge(s_pick_a, i + (layer * NGRP // 4 + 1))
                    for s in range(4):
                        for t in range(GRP):
                            ins = nc.scalar.activation(dist[s % 2][:, t, :], iota[:, :], ACT.Abs, scale=-1.0,
                                                       bias=picks_a[:, GRP * s + t:GRP * s + t + 1])
                        ins.then_inc(s_dist, 1)
                        act.wait_ge(s_dist, 4 * i + (layer * NGRP + s + 1))
                        act.wait_ge(s_grid, 4 * i + (layer * NGRP + s + 1))
                        nc.scalar.activation(oneB[s][:, :, :], dist[s % 2][:, :, :], ACT.Relu, bias=1.0,
                                             scale=-1.0).then_inc(s_oneB, 1)

                act.wait_ge(s_gated, 4 + (layer + 1) * NGRP)

                def split_gated(i, s):
                    nc.scalar.activation(gateH[s % 2][:, :], R[:, ds(4 * i + s, 1), :].rearrange("p a t -> p (a t)"),
                                         ACT.Copy).then_inc(s_gH2, 1)

                split_gated(0, 0)
                with act.Fori(0, 31) as i:
                    for s in range(4):
                        split_gated(i, s + 1)
                        ahead(BASE["v", layer], i, s)
                for s in range(4):
                    if s < 3:
                        split_gated(31, s + 1)
                    if layer < LAYERS - 1 or s < 2:
                        ahead(BASE["v", layer], 31, s)
                act.wait_ge(s_pe, 2 * (BASE["v", layer] + EXP_TILES))
                for tt in range(TT):
                    nc.scalar.activation(otok[:, tt, 0:512], O[2 * tt][:, :], ACT.Copy).then_inc(s_oc, 1)
                for j in range(KT):
                    act.wait_ge(s_res, KT * layer + j + 1)
                    square(j)
                norm(2 * layer + 2)

        @block.vector
        def _(dve):
            steps = [0]

            def step(ins):
                steps[0] += 1
                ins.then_inc(s_vstep, 1)
                return steps[0]

            def after(n):
                dve.wait_ge(s_vstep, n)

            def low_first(base, i, s):
                dve.wait_ge(s_h, 8 * i + (2 * (base + s) + 1))
                nc.vector.tensor_tensor(wL[(2 * s) % 4][:, :], raw[s % RAW][:, 0:HALF],
                                        wH[(2 * s) % 4][:, :].bitcast(fp32), ALU.subtract).then_inc(s_l0, 1)

            def ahead(base, i, s):
                low_first(base, i, s + 2)

            def ada_tile(m, s, turn, chunk, k):
                dve.wait_ge(s_ada[s], 16 * turn)
                a, t, w = acc[:, chunk, :], ada[s][:, :], csT[:, k:k + 1]
                if k == 0:
                    nc.vector.tensor_scalar(a, t, w, None, ALU.mult).then_inc(s_acc, 1)
                else:
                    dve.wait_ge(s_acc, m)
                    nc.vector.scalar_tensor_tensor(a, t, w, a, ALU.mult, ALU.add).then_inc(s_acc, 1)

            def modulations(n, chunks, bank, norms):
                lo, hi = chunks[0] * KT, (chunks[-1] + 1) * KT
                dve.wait_ge(s_modp, n)
                last = step(nc.vector.tensor_tensor(mod[:, lo:hi], bank[:, 0:hi - lo], adab[:, lo:hi], ALU.add))
                after(last)
                for m in norms:
                    gain = (n1, n2)[m % 2]
                    last = step(nc.vector.scalar_tensor_tensor(gs[:, m, :], modcol(m // 2, 3 * (m % 2) + 1), 1.0,
                                                               gain[:, m // 2 * KT:m // 2 * KT + KT], ALU.add, ALU.mult))
                after(last)
                nc.vector.memset(tick[:, 0:1], 0.0).then_inc(s_mod, 1)

            def norm(n):
                dve.wait_ge(s_std, n + 1)
                after(step(nc.vector.reciprocal(rstd[:, :], std[:, :])))

                def scaled(p):
                    nc.vector.tensor_tensor(sq[:, 2 * p:2 * p + 2, :], XT[:, 2 * p:2 * p + 2, :],
                                            rstd[:, None, :].to_broadcast([P, 2, T]), ALU.mult).then_inc(s_xn, 1)

                def low(p):
                    dve.wait_ge(s_hH, 4 * n + p + 1)
                    nc.vector.tensor_tensor(hL[:, 2 * p:2 * p + 2, :], hf[:, 2 * p:2 * p + 2, :],
                                            hH[:, 2 * p:2 * p + 2, :].bitcast(fp32), ALU.subtract).then_inc(s_hin, 1)

                scaled(0)
                scaled(1)
                if n == NORMS - 1:
                    scaled(2)
                    scaled(3)
                else:
                    low(0)
                    scaled(2)
                    low(1)
                    scaled(3)
                    low(2)
                    low(3)

            def residual(layer, chunk, j, bank, half=0):
                return nc.vector.scalar_tensor_tensor(XT[:, j, :], bank[:, half * T:half * T + T],
                                                      modcol(layer, chunk, j, 1), XT[:, j, :], ALU.mult, ALU.add)

            nc.vector.memset(tick[:, 1:2], 0.0).then_inc(s_bank_v, 4)
            nc.vector.memset(tick[:, 2:3], 0.0).then_inc(s_bank_a, 4)
            nc.vector.memset(tick[:, 3:4], 0.0).then_inc(s_gated, 4)
            nc.vector.memset(tick[:, 4:5], 0.0).then_inc(s_grid, 4)
            dve.wait_ge(s_first, 16 * FIRST)
            dve.wait_ge(s_silu, 1)
            for m in range(ADA_FRONT):
                ada_tile(m, m % 4, m // 4 + 1, m // KT, m % KT)
            low_first(0, 0, 0)
            low_first(0, 0, 1)
            modulations(1, (0, 1), ring[0], (0,))
            norm(0)
            dve.wait_ge(s_small, SMALL)
            for layer in range(LAYERS):
                if layer == 0:
                    for t in range(16):
                        ahead(W_V, t // 4, t % 4)
                        m = ADA_FRONT + t
                        ada_tile(m, m % 4, m // 4 + 1, t // KT, t % KT)

                    def gate_tile(f):
                        dve.wait_ge(s_mixed, f + 1)
                        g = f // (SGU_FT // SGU_G)
                        nc.vector.scalar_tensor_tensor(
                            hf[:, f % 8, :].rearrange("p (c t) -> p c t", c=TT),
                            O[f % 4][:, 0:T].rearrange("p (c t) -> p c t", c=TT), vg[:, f:f + 1],
                            bs[:, g:g + 1, :].to_broadcast([P, TT, P]), ALU.mult, ALU.add).then_inc(s_sv, 1)

                    def gate_by(f):
                        dve.wait_ge(s_sv, f + 1)
                        dve.wait_ge(s_bank_a, 4 + SGU_FT + f + 1)
                        nc.vector.tensor_tensor(UV[:, SGU_FT + f, :], hf[:, f % 8, :], UV[:, f, :], ALU.mult)\
                            .then_inc(s_gf, 1)

                    def gated_low(f):
                        dve.wait_ge(s_gH, f + 1)
                        nc.vector.tensor_tensor(gL[:, f, :], UV[:, SGU_FT + f, :], gH[:, f, :].bitcast(fp32),
                                                ALU.subtract).then_inc(s_gL, 1)

                    for t in range(16):
                        ahead(W_U, t // 4, t % 4)
                        if t < ADA_MLP - 16:
                            m = ADA_FRONT + 16 + t
                            ada_tile(m, m % 4, m // 4 + 1, 2, t)
                        if t == 7:
                            dve.wait_ge(s_vc, 8)
                            nc.vector.tensor_reduce(ssum[:, :], ssq[:, :].rearrange("p (c f) -> p c f", c=TT), AX.X,
                                                    ALU.add).then_inc(s_ssq, 1)
                        if t == 8:
                            dve.wait_ge(s_vstd, 1)
                            after(step(nc.vector.reciprocal(ssum[:, :], vstd[:, :])))
                            for c in range(TT):
                                nc.vector.tensor_scalar(vtok[:, c, :], vtok[:, c, :], ssum[:, c:c + 1], None, ALU.mult)\
                                    .then_inc(s_vn, 1)
                        if t == 9:
                            modulations(2, (2, 3, 4), O[3], (1,))
                        if t > 9:
                            f = 2 * (t - 10)
                            gate_tile(f)
                            gate_tile(f + 1)
                            gate_by(f)
                            gate_by(f + 1)
                        if t > 11:
                            gated_low(2 * (t - 12))
                            gated_low(2 * (t - 12) + 1)
                    for f in range(12, SGU_FT):
                        gate_tile(f)
                        gate_by(f)
                        gated_low(f - 4)
                    for f in range(12, SGU_FT):
                        gated_low(f)
                    for j in range(KT):
                        for s in range(2):
                            ahead(W_OUT, j // 2, 2 * (j % 2) + s)
                        dve.wait_ge(s_pe, 2 * (W_OUT + 2 * j + 2))
                        residual(0, 2, j, ring[j % 4]).then_inc(s_bank_v, 1)
                else:
                    base = BASE["p_in", 1]
                    W = PAD + T + PAD
                    lev = [hf[:, :, :].rearrange("p a b -> p (a b)")[:, a * 2 * W:(a + 1) * 2 * W]
                           .rearrange("p (c w) -> p c w", c=2) for a in range(2)]
                    place, hi_t, lo_t = UV[:, 12, :], UV[:, 13, :], UV[:, 14, :]
                    after(step(nc.vector.memset(Z[:, :, 0:PAD], 0.0)))
                    after(step(nc.vector.memset(Z[:, :, PAD + T:], 0.0)))
                    for j in range(KT):
                        ahead(base, j // 4, j % 4)
                        if j == 0:
                            step(nc.vector.tensor_scalar(UV[:, 12, 0:P], iota[:, :], 0.0, None, ALU.add))
                            after(step(nc.vector.tensor_scalar(UV[:, 12, P:T], iota[:, :], float(P), None, ALU.add)))
                        f = POOL_ORDER[j]
                        g = f // 2
                        if j % 2 == 0:
                            half = float(1 << g)
                            step(nc.vector.tensor_scalar(hi_t, place, half, float(T), ALU.add, ALU.min))
                            after(step(nc.vector.tensor_scalar(lo_t, place, -half, 0.0, ALU.add, ALU.max)))
                            after(step(nc.vector.tensor_tensor(hi_t, hi_t, lo_t, ALU.subtract)))
                            after(step(nc.vector.reciprocal(UV[:, 8 + g, :], hi_t)))
                        dve.wait_ge(s_pe, 2 * (base + j + 1))
                        nc.vector.tensor_copy(Z[:, f, PAD:PAD + T], ring[j % 4][:, 0:T]).then_inc(s_bank_v, 1)
                        if j % 2 == 0:
                            continue
                        dve.wait_ge(s_bank_v, 4 + KT + j + 1)
                        z2 = Z[:, 2 * g:2 * g + 2, :]
                        after(step(nc.vector.tensor_tensor(lev[0][:, :, 1:W - 1], z2[:, :, 0:W - 2], z2[:, :, 1:W - 1],
                                                           ALU.add)))
                        lo, hi, cur = 1, W - 1, 0
                        for m in range(1, g + 1):
                            r = 1 << (m - 1)
                            lo, hi = lo + r, hi - r
                            after(step(nc.vector.tensor_tensor(lev[1 - cur][:, :, lo:hi], lev[cur][:, :, lo - r:hi - r],
                                                               lev[cur][:, :, lo + r:hi + r], ALU.add)))
                            cur = 1 - cur
                        pooled = vtok[:, 0, 2 * g * T:(2 * g + 2) * T].rearrange("p (c t) -> p c t", c=2)
                        after(step(nc.vector.tensor_tensor(pooled, lev[cur][:, :, PAD:PAD + T],
                                                           UV[:, 8 + g:9 + g, :].to_broadcast([P, 2, T]), ALU.mult)))
                        nc.vector.tensor_tensor(pooled, pooled, z2[:, :, PAD:PAD + T], ALU.subtract).then_inc(s_pooled, 1)

                    def pooled_low(n):
                        f = POOL_ORDER[n]
                        dve.wait_ge(s_gH, SGU_FT + n + 1)
                        nc.vector.tensor_tensor(gL[:, f, :], UV[:, SGU_FT + f, :], gH[:, f, :].bitcast(fp32),
                                                ALU.subtract).then_inc(s_gL, 1)

                    for n, f in enumerate(POOL_ORDER):
                        dve.wait_ge(s_pg, n + 1)
                        nc.vector.tensor_scalar(UV[:, SGU_FT + f, :], pool_bank(n)[:, 0:T], ps[:, f:f + 1], None,
                                                ALU.mult).then_inc(s_gf, 1)
                        if n > 1:
                            pooled_low(n - 2)
                    pooled_low(KT - 2)
                    pooled_low(KT - 1)
                    base = BASE["p_out", 1]
                    for j in range(KT):
                        ahead(base, j // 4, j % 4)
                        dve.wait_ge(s_pe, 2 * (base + j + 1))
                        residual(1, 2, j, ring[j % 4]).then_inc(s_bank_v, 1)
                norm(2 * layer + 1)
                for t in range(16):
                    ahead(BASE["w_q", layer], t // 4, t % 4)
                    if t % 4 == 2 and t > 4:
                        b = t // 4 - 1
                        for tt in range(TT):
                            dve.wait_ge(s_sc, 8 * layer + 2 * b + tt + 1)
                            nc.vector.tensor_copy(S[:, tt, 4 * b:4 * b + 4, :],
                                                  score_bank(b, tt)[:, :].rearrange("p (a n) -> p a n", a=4))\
                                .then_inc(s_scc, 1)

                def top16(values, out_v, out_i):
                    after(step(nc.vector.max(out_v[:, 0:8], values)))
                    a = step(nc.vector.max_index(out_i[:, 0:8], out_v[:, 0:8], values))
                    after(a)
                    after(step(nc.vector.match_replace(values, out_v[:, 0:8], values, -3.0e38)))
                    after(step(nc.vector.max(out_v[:, 8:16], values)))
                    return step(nc.vector.max_index(out_i[:, 8:16], out_v[:, 8:16], values))

                def topk_step(n):
                    if n == 0:
                        for tt in range(TT):
                            dve.wait_ge(s_sc, 8 * layer + 6 + tt + 1)
                            nc.vector.tensor_copy(S[:, tt, 12:16, :],
                                                  score_bank(3, tt)[:, :].rearrange("p (a n) -> p a n", a=4))\
                                .then_inc(s_scc, 1)
                        dve.wait_ge(s_scc, 8 * layer + 8)
                    elif n < 23:
                        for m in ((3 * (n - 1)) // 2, (3 * (n - 1)) // 2 + 1)[:1 + (n - 1) % 2]:
                            if m < 32:
                                top16(S[:, m // 16, m % 16, :], top_v[:, m // 16, m % 16, :], top_i[:, m // 16, m % 16, :])
                    elif n < 39:
                        tt, h = (n - 23) // 8, (n - 23) % 8
                        if h == 0:
                            after(steps[0])
                            v = top_v[:, tt, :, :].rearrange("p (h s) k -> p h s k", s=2)
                            after(step(nc.vector.tensor_tensor(
                                C[:, :, :].rearrange("p h (a b) -> p h a b", a=TOPK),
                                v[:, :, 0, :, None].to_broadcast([P, HEADS, TOPK, TOPK]),
                                v[:, :, 1, None, :].to_broadcast([P, HEADS, TOPK, TOPK]), ALU.add)))
                        top16(C[:, h, :], best[:, tt, h, :], pos[:, tt, h, :])
                    elif n == 39:
                        after(steps[0])
                        flat = pos[:, :, :, :].rearrange("p t h k -> p t (h k)")
                        step(nc.vector.tensor_scalar(pos_ab[:, 0], flat, 4, None, ALU.logical_shift_right))
                        step(nc.vector.tensor_scalar(pos_ab[:, 1], flat, 15, None, ALU.bitwise_and))
                        b = best[:, :, :, :].rearrange("p t h k -> p (t h) k")
                        nc.vector.tensor_tensor(ex[:, :, :, :].rearrange("p t h k -> p (t h) k"), b,
                                                b[:, :, 0:1].to_broadcast([P, TT * HEADS, TOPK]),
                                                ALU.subtract).then_inc(s_diff, 1)
                        after(steps[0])
                    elif n == 40:
                        step(nc.vector.tensor_copy(ab[:, :, :, :], pos_ab[:, :, :, :]))
                        step(nc.vector.tensor_copy(top_f[:, :, :, :], top_i[:, :, :, :]))
                        after(steps[0])
                    elif n < 65:
                        tt, side, hh, what = (n - 41) // 12, (n - 41) // 6 % 2, (n - 41) // 3 % 2, (n - 41) % 3
                        half = HK // 2
                        if what == 0:
                            after(step(nc.vector.tensor_tensor(
                                M[:, :, :], ab[:, side, tt, hh * half:hh * half + half, None].to_broadcast([P, half, TOPK]),
                                iota_k[:, None, :].to_broadcast([P, half, TOPK]), ALU.is_equal)))
                        elif what == 1:
                            keys_of = top_f[:, tt, :, :].rearrange("p (h s) k -> p h s k", s=2)[:, 4 * hh:4 * hh + 4, side, None, :]
                            m4 = M[:, :, :].rearrange("p (h k) a -> p h k a", h=4)
                            after(step(nc.vector.tensor_tensor(m4, m4, keys_of.to_broadcast([P, 4, TOPK, TOPK]), ALU.mult)))
                        else:
                            after(step(nc.vector.tensor_reduce(sel[:, side, tt, hh * half:hh * half + half], M[:, :, :],
                                                               AX.X, ALU.add)))
                    else:
                        dve.wait_ge(s_exp, layer + 1)
                        b = best[:, :, :, :].rearrange("p t h k -> p (t h) k")
                        after(step(nc.vector.tensor_reduce(zsum[:, :], b, AX.X, ALU.add)))
                        after(step(nc.vector.reciprocal(zsum[:, :], zsum[:, :])))
                        nc.vector.tensor_tensor(sel[:, 2, :, :].rearrange("p t (h k) -> p (t h) k", h=HEADS), b,
                                                zsum[:, :, None].to_broadcast([P, TT * HEADS, TOPK]), ALU.mult)\
                            .then_inc(s_sel, 1)

                base = BASE["u", layer]
                TOPK_STEPS = 66
                for n in range(68):
                    ahead(base, n // 4, n % 4)
                    if n < TOPK_STEPS:
                        topk_step(n)
                with dve.Fori(68 // 4, 128 // 4) as i:
                    for s in range(4):
                        ahead(base, i, s)

                dve.wait_ge(s_selT, layer + 1)
                for a in range(3):
                    nc.vector.tensor_copy(selT[:, a, :], O[a][:, 0:T]).then_inc(s_selc, 1)
                dve.wait_ge(s_selc, 3 * (layer + 1))
                dve.wait_ge(s_bank_a, 4 + ACT_EVACS + ACT_PER_LAYER * (layer + 1))

                with dve.Fori(0, NGRP // 4) as i:
                    nc.vector.tensor_copy(picks[:, :, :], selT[:, :, ds(4 * GRP * i, 4 * GRP)]).then_inc(s_pick, 1)
                    dve.wait_ge(s_pick, i + (layer * NGRP // 4 + 1))
                    for s in range(4):
                        for t in range(GRP):
                            c = GRP * s + t
                            ins = nc.vector.tensor_scalar(oneA[s][:, t, :], iota[:, :], picks[:, 0, c:c + 1],
                                                          picks[:, 2, c:c + 1], ALU.is_equal, ALU.mult)
                        ins.then_inc(s_oneA, 1)
                    for s in range(4):
                        dve.wait_ge(s_grid, 4 * i + (4 + layer * NGRP + s + 1))
                        r = R[:, :, ds(GRP * (4 * i + s), GRP)]
                        nc.vector.tensor_tensor(r, ring[s][:, :].rearrange("p (t n) -> p n t", t=GRP), r, ALU.mult)\
                            .then_inc(s_gated, 1)
                dve.wait_ge(s_gated, 4 + (layer + 1) * NGRP)

                def split_gated(i, s):
                    dve.wait_ge(s_gH2, 4 * i + (layer * EXP_TILES + s + 1))
                    nc.vector.tensor_tensor(gateL[s % 2][:, :], R[:, ds(4 * i + s, 1), :].rearrange("p a t -> p (a t)"),
                                            gateH[s % 2][:, :].bitcast(fp32), ALU.subtract).then_inc(s_gL2, 1)

                base = BASE["v", layer]
                split_gated(0, 0)
                with dve.Fori(0, (ADA_FROM if layer == 0 else 124) // 4) as i:
                    for s in range(4):
                        split_gated(i, s + 1)
                        ahead(base, i, s)
                if layer == 0:
                    for n in range(ADA_FROM, EXP_TILES):
                        if n < EXP_TILES - 1:
                            split_gated(n // 4, n % 4 + 1)
                        ahead(base, n // 4, n % 4)
                        t = n - ADA_FROM
                        m = ADA_FRONT + ADA_MLP + t
                        ada_tile(m, m % 4, m // 4 + 1, t // KT, t % KT)
                    modulations(3, tuple(range(5, 12)), ring[3], (2, 3))
                else:
                    for s in range(4):
                        if s < 3:
                            split_gated(31, s + 1)
                        if s < 2:
                            ahead(base, 31, s)
                dve.wait_ge(s_pe, 2 * (base + EXP_TILES))
                for tt in range(TT):
                    nc.vector.tensor_copy(otok[:, tt, 512:1024], O[2 * tt + 1][:, :]).then_inc(s_oc, 1)
                for j in range(KT):
                    if j % 2 == 0:
                        dve.wait_ge(s_ot, layer * 4 + j // 2 + 1)
                    residual(layer, 5, j, ring[j // 2], j % 2).then_inc(s_res, 1)
                norm(2 * layer + 2)

        @block.tensor
        def _(pe):
            mm = nc.tensor.matmul

            def tile_product(base, i, s, bank, xH, xL, k0=0, first=True, last=True, pairs=None):
                for half in range(2):
                    pe.wait_ge((s_l0, s_l1)[half], 4 * i + (base + s + 1))
                    slot = (2 * s + half) % 4
                    for kk in range(4):
                        k = 4 * half + kk
                        if pairs and k % 2 == 0:
                            pe.wait_ge(pairs[0], pairs[1] + k // 2 + 1)
                        a, b = wH[slot][:, kk * P:kk * P + P], wL[slot][:, kk * P:kk * P + P]
                        mm(bank[:, 0:T], a, xH[:, k0 + k, :], start=(first and k == 0), stop=False)
                        mm(bank[:, 0:T], a, xL[:, k0 + k, :], start=False, stop=False)
                        ins = mm(bank[:, 0:T], b, xH[:, k0 + k, :], start=False, stop=(last and k == KT - 1))
                    ins.then_inc(s_pe, 1)

            def stage(name, layer, emptied, before, lo=0, hi=None, norm_n=None):
                base = BASE[name, layer]
                tiles = {n: t for n, l, t in STREAM}[name]
                with pe.Fori(lo // 4, (tiles if hi is None else hi) // 4) as i:
                    for s in range(4):
                        pe.wait_ge(emptied, 4 * i + (before + s + 1))
                        tile_product(base, i, s, ring[s], hH, hL,
                                     pairs=(s_hin, 4 * norm_n) if norm_n is not None and s == 0 else None)

            def mean(n, j):
                pe.wait_ge(s_sq, KT * n + j + 1)
                ins = mm(O[0][:, 0:T], mean_w[:, :], sq[:, j, :], start=(j == 0), stop=(j == KT - 1))
                if j == KT - 1:
                    ins.then_inc(s_ms, 1)

            def modulations(chunks, summed, bank):
                pe.wait_ge(s_acc, summed)
                for x in range(chunks):
                    for j in range(KT):
                        ins = mm(bank[:, KT * x + j:KT * x + j + 1], acc[:, x, j * P:j * P + P], ones[:, :],
                                 start=True, stop=True)
                ins.then_inc(s_modp, 1)

            def mix_tile(f):
                if f == 0:
                    pe.wait_ge(s_vn, TT)
                if f >= 4:
                    pe.wait_ge(s_sv, f - 3)
                for c in range(TT):
                    ins = mm(O[f % 4][:, c * P:c * P + P], vtok[:, c, f * P:f * P + P],
                             ws[:, f // (SGU_FT // SGU_G), :], start=True, stop=True)
                ins.then_inc(s_mixed, 1)

            def group_product(n):
                f = POOL_ORDER[n]
                pe.wait_ge(s_pooled, n // 2 + 1)
                if n >= 4:
                    pe.wait_ge(s_gf, SGU_FT + n - 3)
                wg = UV[:, 0:8, :].rearrange("p a b -> p (a b)")
                for kk in range(2):
                    at, k = (2 * f + kk) * P, f // 2 * 2 + kk
                    ins = mm(pool_bank(n)[:, 0:T], wg[:, at:at + P], vtok[:, 0, k * T:k * T + T],
                             start=(kk == 0), stop=(kk == 1))
                ins.then_inc(s_pg, 1)

            def scores(layer, j):
                pe.wait_ge(s_bank_a, 4 + ACT_EVACS + ACT_PER_LAYER * layer + j + 1)
                b = j // 4
                if b > 1 and j % 4 == 0:
                    pe.wait_ge(s_scc, 8 * layer + 2 * (b - 1))
                for tt in range(TT):
                    ins = mm(score_bank(b, tt)[:, j % 4 * P:j % 4 * P + P], UV[:, j, tt * P:tt * P + P],
                             keys[:, j % 2, j // 2, :], start=True, stop=True)
                    if j % 4 == 3:
                        ins.then_inc(s_sc, 1)

            pe.wait_ge(s_const, 7)
            for j in range(KT):
                mean(0, j)
            modulations(2, ADA_FRONT, ring[0])
            pe.wait_ge(s_mod, 1)
            pe.wait_ge(s_small, SMALL)
            for layer in range(LAYERS):
                if layer == 0:
                    stage("w_v", 0, s_bank_a, 0, norm_n=0)
                    for t in range(16):
                        pe.wait_ge(s_bank_a, 16 + t + 1)
                        tile_product(W_U, t // 4, t % 4, ring[t % 4], hH, hL)
                        if t < 8:
                            c, f = t // 4, t % 4
                            if t == 0:
                                pe.wait_ge(s_bank_a, 4 + 16)
                            if t >= 4:
                                pe.wait_ge(s_vc, t - 3)
                            for q in range(4):
                                ins = nc.tensor.transpose(O[f][:, q * P:q * P + P],
                                                          UV[:, SGU_FT + 4 * f + q, c * P:c * P + P], ident[:, :])
                            ins.then_inc(s_vt, 1)
                        if t == 8:
                            pe.wait_ge(s_vc, 8)
                            modulations(3, ADA_FRONT + ADA_MLP, O[3])
                        if t == 10:
                            pe.wait_ge(s_mod, 2)
                        if t > 9:
                            mix_tile(2 * (t - 10))
                            mix_tile(2 * (t - 10) + 1)
                    for f in range(12, SGU_FT):
                        mix_tile(f)
                    for j in range(KT):
                        pe.wait_ge(s_bank_v, j + 1)
                        if j == 0:
                            pe.wait_ge(s_gL, KT)
                        for kk in range(2):
                            if (j, kk) == (0, 1):
                                pe.wait_ge(s_gL, SGU_FT)
                            tile_product(W_OUT, j // 2, 2 * (j % 2) + kk, ring[j % 4], gH, gL, KT * kk,
                                         first=(kk == 0), last=(kk == 1))
                        if j > 1:
                            mean(1, j - 2)
                else:
                    for j in range(KT):
                        pe.wait_ge(s_bank_v, KT + j + 1)
                        tile_product(BASE["p_in", 1], j // 4, j % 4, ring[j % 4], hH, hL,
                                     pairs=(s_hin, 8) if j == 0 else None)
                        if j == 4:
                            pe.wait_ge(s_late, 48)
                        if j > 3 and j % 2 == 0:
                            group_product(j - 4)
                            group_product(j - 3)
                    for n in range(4, KT):
                        group_product(n)
                    pe.wait_ge(s_gL, SGU_FT + KT)
                    for j in range(KT):
                        pe.wait_ge(s_bank_v, 2 * KT + j + 1)
                        tile_product(BASE["p_out", 1], j // 4, j % 4, ring[j % 4], gH, gL)
                        if j > 1:
                            mean(3, j - 2)
                n = 2 * layer + 1
                mean(n, KT - 2)
                mean(n, KT - 1)
                for t in range(17):
                    if t < 16:
                        pe.wait_ge(s_bank_a, ACT_EVACS + ACT_PER_LAYER * layer + t + 1)
                        tile_product(BASE["w_q", layer], t // 4, t % 4, ring[t % 4], hH, hL,
                                     pairs=(s_hin, 4 * n) if t == 0 else None)
                    if t > 0:
                        scores(layer, t - 1)
                stage("u", layer, s_bank_a, ACT_EVACS + ACT_PER_LAYER * layer + 16)
                pe.wait_ge(s_sel, layer + 1)
                for a in range(3):
                    for tt in range(TT):
                        ins = nc.tensor.transpose(O[a][:, tt * P:tt * P + P], sel[:, a, tt, :], ident[:, :])
                ins.then_inc(s_selT, 1)
                pe.wait_ge(s_bank_a, 4 + ACT_EVACS + ACT_PER_LAYER * (layer + 1))
                with pe.Fori(0, NGRP // 4) as i:
                    for s in range(4):
                        pe.wait_ge(s_oneA, 4 * i + (layer * NGRP + s + 1))
                        pe.wait_ge(s_oneB, 4 * i + (layer * NGRP + s + 1))
                        pe.wait_ge(s_gated, 4 * i + (layer * NGRP + s + 1))
                        for t in range(GRP):
                            ins = mm(ring[s][:, t * KEYS:(t + 1) * KEYS], oneB[s][:, t, :], oneA[s][:, t, :],
                                     start=True, stop=True)
                        ins.then_inc(s_grid, 1)

                base = BASE["v", layer]

                def values(i, s, first=False, last=False):
                    pe.wait_ge(s_gL2, 4 * i + (layer * EXP_TILES + s + 1))
                    for half in range(2):
                        pe.wait_ge((s_l0, s_l1)[half], 4 * i + (base + s + 1))
                        slot = (2 * s + half) % 4
                        for tt in range(TT):
                            o = O[2 * tt + half]
                            a = gateH[s % 2][:, tt * P:tt * P + P]
                            b = gateL[s % 2][:, tt * P:tt * P + P]
                            mm(o[:, :], a, wH[slot][:, :], start=first, stop=False)
                            mm(o[:, :], a, wL[slot][:, :], start=False, stop=False)
                            ins = mm(o[:, :], b, wH[slot][:, :], start=False, stop=last)
                        ins.then_inc(s_pe, 1)

                for s in range(4):
                    values(0, s, first=(s == 0))
                with pe.Fori(1, 31) as i:
                    for s in range(4):
                        values(i, s)
                for s in range(4):
                    values(31, s, last=(s == 3))
                if layer == 0:
                    pe.wait_ge(s_gated, 4 + NGRP)
                    modulations(7, ADA_FRONT + ADA_MLP + ADA_V, ring[3])
                    pe.wait_ge(s_mod, 3)
                pe.wait_ge(s_oc, 4 * (layer + 1))
                for j in range(KT):
                    for tt in range(TT):
                        ins = nc.tensor.transpose(ring[j // 2][:, (j % 2) * T + tt * P:(j % 2) * T + tt * P + P],
                                                  otok[:, tt, j * P:j * P + P], ident[:, :])
                    if j % 2:
                        ins.then_inc(s_ot, 1)
                for j in range(KT):
                    mean(2 * layer + 2, j)


def tiles_of(w, n_in):
    n = w.shape[-1]
    w = w.reshape(n_in, KT, P, n // P, P).transpose(3, 0, 2, 1, 4)
    return np.ascontiguousarray(w.reshape(n // P * n_in, P, KT * P))


def kernel(**inputs):
    import concourse.bacc as bacc
    from concourse.bass_utils import run_bass_kernel_spmd

    a = {k: np.asarray(v) for k, v in inputs.items()}

    def cols(w):
        return np.ascontiguousarray(w.reshape(-1, P).T)

    arrays = {
        "xt": np.ascontiguousarray(a["x"][0].reshape(T, KT, P).transpose(2, 1, 0)),
        "c": cols(a["c"]),
        "ada": np.ascontiguousarray(a["ada_w"].reshape(LAYERS, KT, P, CHUNKS, D).transpose(0, 3, 1, 2, 4)
                                    .reshape(LAYERS * CHUNKS * KT, P, D)),
        "adab": cols(a["ada_b"]),
        "n1": cols(a["norm1_g"]),
        "n2": cols(a["norm2_g"]),
        "fg": cols(a["final_gain"]),
        "w_in": tiles_of(a["sgu_w_in"][0], 1),
        "vg": cols(a["sgu_v_gain"]),
        "ws": np.ascontiguousarray(a["sgu_w_s"][0].transpose(2, 0, 1)),
        "bs": np.ascontiguousarray(np.broadcast_to(a["sgu_b_s"][0], (P, SGU_G, P))),
        "w_out": tiles_of(a["sgu_w_out"][0], 2),
        "p_in": tiles_of(a["pool_w_in"][0], 1)[POOL_ORDER],
        "p_grp": np.ascontiguousarray(
            a["pool_w_grp"][0].reshape(PG, 2, P, 2, P).transpose(2, 0, 3, 1, 4).reshape(P, 8, T)),
        "ps": cols(a["pool_scale"]),
        "p_out": tiles_of(a["pool_w_out"][0], 1),
        "w_q": np.stack([tiles_of(a["peer_w_q"][i], 1) for i in range(LAYERS)]),
        "k1": np.ascontiguousarray(a["peer_k1"].transpose(0, 3, 1, 2)),
        "k2": np.ascontiguousarray(a["peer_k2"].transpose(0, 3, 1, 2)),
        "u": np.ascontiguousarray(a["peer_u"].reshape(LAYERS, EXP_TILES, P, KT, P).transpose(0, 1, 4, 3, 2)
                                  .reshape(LAYERS, EXP_TILES, P, KT * P)),
        "v": a["peer_v"].reshape(LAYERS, EXP_TILES, P, D),
    }
    nc = bacc.Bacc("TRN2", target_bir_lowering=False, num_devices=1)
    args = [nc.dram_tensor(f"in_{k}", v.shape, mybir.dt.from_np(v.dtype), kind="ExternalInput").ap()
            for k, v in arrays.items()]
    out = nc.dram_tensor("out_t", (P, KT, T), mybir.dt.float32, kind="ExternalOutput").ap()
    build(nc, *args, out)
    r = run_bass_kernel_spmd(nc, [{f"in_{k}": v for k, v in arrays.items()}], core_ids=[0])
    return r.results[0]["out_t"].transpose(2, 1, 0).reshape(1, T, D)
```

```python
from contextlib import ExitStack

import concourse.bass as bass
import numpy as np
from concourse import mybir

P = 128
D = 1024
KT = D // P
T = 256
TT = T // P
LAYERS = 2
CHUNKS = 6
EPS = 1e-6
SGU_W = 2048
SGU_FT = SGU_W // P
SGU_G = 8
HEADS = 8
KEYS = 128
TOPK = 16
HK = HEADS * TOPK
PG = 4
PAD = 8
EXP_TILES = KEYS
RAW = 4
BANKS = 4
HALF = 512
ADA_AT = 32
BAND = KEYS // 2
GRP = 8
NGRP = T // GRP
PAIRS = NGRP // 2

POOL_ORDER = [6, 7, 4, 5, 2, 3, 0, 1]

STREAM = [("w_v", 0, 16), ("w_u", 0, 16), ("w_out", 0, 16), ("w_q", 0, 16), ("u", 0, EXP_TILES), ("v", 0, EXP_TILES),
          ("p_in", 1, 8), ("p_out", 1, 8), ("w_q", 1, 16), ("u", 1, EXP_TILES), ("v", 1, EXP_TILES)]
BASE = {}
TOTAL = 0
for _name, _layer, _tiles in STREAM:
    BASE[_name, _layer] = TOTAL
    TOTAL += _tiles


def build(nc, xt_d, c_d, ada_d, adab_d, n1_d, n2_d, fg_d, w_in_d, vg_d, ws_d, bs_d, w_out_d, p_in_d, p_grp_d,
          ps_d, p_out_d, w_q_d, k1_d, k2_d, u_d, v_d, out_d):
    fp32, f32r, bf16, u32 = mybir.dt.float32, mybir.dt.float32r, mybir.dt.bfloat16, mybir.dt.uint32
    ALU, ACT, AX = mybir.AluOpType, mybir.ActivationFunctionType, mybir.AxisListType
    ds = bass.ds

    stream_dram = {("w_v", 0): w_in_d[SGU_FT:2 * SGU_FT], ("w_u", 0): w_in_d[0:SGU_FT], ("w_out", 0): w_out_d,
                   ("p_in", 1): p_in_d, ("p_out", 1): p_out_d}
    for layer in range(LAYERS):
        stream_dram["w_q", layer] = w_q_d[layer]
        stream_dram["u", layer] = u_d[layer]
        stream_dram["v", layer] = v_d[layer]

    ctx = ExitStack()
    with ctx:
        def sb(name, shape, dt=fp32, at=None):
            return (at or ctx).enter_context(nc.sbuf_tensor(name, shape, dt))

        def sem(name):
            return ctx.enter_context(nc.semaphore(name))

        XT = sb("XT", [P, KT, T])
        raw = [sb(f"raw{s}", [P, KT * P]) for s in range(RAW)]
        wH = [sb(f"wH{s}", [P, HALF], f32r) for s in range(4)]
        wL = [sb(f"wL{s}", [P, HALF], f32r) for s in range(4)]
        hH = sb("hH", [P, KT, T], f32r)
        hL = sb("hL", [P, KT, T], f32r)
        gateH = [sb(f"gateH{x}", [P, T], f32r) for x in range(2)]
        gateL = [sb(f"gateL{x}", [P, T], f32r) for x in range(2)]
        oneB = [sb(f"oneB{x}", [P, KEYS, GRP], bf16) for x in range(2)]
        with ExitStack() as one:
            rstd = sb("rstd", [P, T], at=one)
            std = sb("std", [P, T], at=one)
            sel = sb("sel", [P, 3, TT, HK], at=one)
        with ExitStack() as one:
            gate_rest = sb("gate_rest", [P, T], at=one)
            oneE = sb("oneE", [P, BAND, GRP], bf16, at=one)
            oneA0 = sb("oneA0", [P, 3, BAND, GRP], bf16, at=one)
        shared = sb("shared", [P, 2 * T + 3 * TT * HK])
        oneA = [oneA0, sb("oneA1", [P, 3, BAND, GRP], bf16)]
        iota_g = sb("iota_g", [P, KEYS, GRP], bf16)
        mod = sb("mod", [P, LAYERS * CHUNKS * KT])
        adab = sb("adab", [P, LAYERS * CHUNKS * KT])
        n1 = sb("n1", [P, LAYERS * KT])
        n2 = sb("n2", [P, LAYERS * KT])
        fg = sb("fg", [P, KT])
        vg = sb("vg", [P, SGU_FT])
        ps = sb("ps", [P, KT])
        csT = sb("csT", [P, KT])
        gs = sb("gs", [P, 5, KT])
        eps = sb("eps", [P, 1])
        mean_w = sb("mean_w", [P, P])
        ident = sb("ident", [P, P])
        iota = sb("iota", [P, KEYS])
        tick = sb("tick", [P, 8])
        ssq = sb("ssq", [P, 8])
        ssum = sb("ssum", [P, TT])
        vstd = sb("vstd", [P, TT])
        ones = sb("ones", [P, 1])
        ones_b = sb("ones_b", [P, 1], bf16)
        selT = sb("selT", [P, 5, T], bf16)

        with ExitStack() as mix:
            UV = sb("UV", [P, 32, T], at=mix)
            gH = sb("gH", [P, SGU_FT, T], f32r, at=mix)
            gL = sb("gL", [P, SGU_FT, T], f32r, at=mix)
            vtok = sb("vtok", [P, TT, SGU_W], at=mix)
            sq = sb("sq", [P, KT, T], at=mix)
            hf = sb("hf", [P, KT, T], at=mix)
            bs = sb("bs", [P, SGU_G, P], at=mix)
            ws = sb("ws", [P, SGU_G, P], at=mix)
            keys = sb("keys", [P, 2, HEADS, KEYS], at=mix)
            Z = sb("Z", [P, KT, PAD + T + PAD], at=mix)
        with ExitStack() as ad:
            sb("under_ada", [P, ADA_AT * T], at=ad)
            ada = [sb(f"ada{x}", [P, D], at=ad) for x in range(4)]
            acc = sb("acc", [P, 3, D], at=ad)
        with ExitStack() as ad:
            ada_v = [sb(f"ada_v{x}", [P, D], at=ad) for x in range(4)]
            acc_v = sb("acc_v", [P, 7, D], at=ad)
            parts_v = sb("parts_v", [P, 7, 3, D], bf16, at=ad)
        with ExitStack() as ad:
            sb("under_parts_m", [P, 112 * T], at=ad)
            parts_m = sb("parts_m", [P, 2, 3, D], bf16, at=ad)
        with ExitStack() as tk:
            sb("under_topk", [P, 80 * T], at=tk)
            S = sb("S", [P, TT, 2 * HEADS, KEYS], at=tk)
            top_v = sb("top_v", [P, TT, 2 * HEADS, TOPK], at=tk)
            top_i = sb("top_i", [P, TT, 2 * HEADS, TOPK], u32, at=tk)
            top_f = sb("top_f", [P, TT, 2 * HEADS, TOPK], at=tk)
            best = sb("best", [P, TT, HEADS, TOPK], at=tk)
            C = sb("C", [P, HEADS, TOPK * TOPK], at=tk)
            M = sb("M", [P, HK // 2, TOPK], at=tk)
            pos = sb("pos", [P, TT, HEADS, TOPK], u32, at=tk)
            pos_ab = sb("pos_ab", [P, 2, TT, HK], u32, at=tk)
            ab = sb("ab", [P, 2, TT, HK], at=tk)
            ex = sb("ex", [P, TT, HEADS, TOPK], at=tk)
            zsum = sb("zsum", [P, TT * HEADS], at=tk)
        with ExitStack() as rr:
            R = sb("R", [P, EXP_TILES, T], at=rr)
        with ExitStack() as oo:
            sb("under_otok", [P, 88 * T], at=oo)
            otok = sb("otok", [P, TT, D], at=oo)

        ring = [ctx.enter_context(nc.psum_tensor(f"ring{b}", [P, 512], fp32)) for b in range(BANKS)]
        O = [ctx.enter_context(nc.psum_tensor(f"O{b}", [P, 512], fp32)) for b in range(4)]

        s_first = sem("s_first")
        s_x = sem("s_x")
        s_keys = sem("s_keys")
        s_small = sem("s_small")
        s_const = sem("s_const")
        s_silu = sem("s_silu")
        s_ada = [sem(f"s_ada{x}") for x in range(4)]
        s_acc = sem("s_acc")
        s_acc2 = sem("s_acc2")
        s_modp = sem("s_modp")
        s_mod = sem("s_mod")
        s_raw = [sem(f"s_raw{x}") for x in range(RAW)]
        s_h = sem("s_h")
        s_l0 = sem("s_l0")
        s_l1 = sem("s_l1")
        s_pe = sem("s_pe")
        s_bank_a = sem("s_bank_a")
        s_bank_v = sem("s_bank_v")
        s_res = sem("s_res")
        s_sq = sem("s_sq")
        s_ms = sem("s_ms")
        s_std = sem("s_std")
        s_xn = sem("s_xn")
        s_hf = sem("s_hf")
        s_hH = sem("s_hH")
        s_hin = sem("s_hin")
        s_vt = sem("s_vt")
        s_vc = sem("s_vc")
        s_ssq = sem("s_ssq")
        s_vstd = sem("s_vstd")
        s_vn = sem("s_vn")
        s_mixed = sem("s_mixed")
        s_sv = sem("s_sv")
        s_gf = sem("s_gf")
        s_gH = sem("s_gH")
        s_gL = sem("s_gL")
        s_sc = sem("s_sc")
        s_scc = sem("s_scc")
        s_diff = sem("s_diff")
        s_exp = sem("s_exp")
        s_sel = sem("s_sel")
        s_selT = sem("s_selT")
        s_eq = sem("s_eq")
        s_one = sem("s_one")
        s_grid = sem("s_grid")
        s_gated = sem("s_gated")
        s_gH2 = sem("s_gH2")
        s_gL2 = sem("s_gL2")
        s_oc_a = sem("s_oc_a")
        s_oc_v = sem("s_oc_v")
        s_ot = sem("s_ot")
        s_pooled = sem("s_pooled")
        s_pg = sem("s_pg")
        s_late = sem("s_late")
        s_vstep = sem("s_vstep")
        s_out = sem("s_out")

        block = ctx.enter_context(nc.Block())

        def pool_bank(n):
            return O[n % 4]

        def score_bank(b, tt):
            return O[2 * (b % 2) + tt]

        def modcol(layer, chunk, j=0, n=KT):
            at = (layer * CHUNKS + chunk) * KT + j
            return mod[:, at:at + n]

        first_loads = [(csT[:, :], c_d), (adab[:, :], adab_d), (n1[:, :], n1_d)]
        small_loads = [(n2[:, :], n2_d), (fg[:, :], fg_d), (vg[:, :], vg_d), (ps[:, :], ps_d), (bs[:, :, :], bs_d),
                       (ws[:, :, :], ws_d)]
        FIRST, SMALL = 16 * len(first_loads), 16 * len(small_loads)
        NORMS = 2 * LAYERS + 1
        ADA_FRONT, ADA_MLP, ADA_V = 2 * KT, 3 * KT, 7 * KT
        ADA_EARLY = 9
        ADA_SPANS = ((24, 60, 0), (64, 112, 3))
        ADA_SLOTS = tuple(s for s in range(12) if s % 3 < 2)
        W_V, W_U, W_OUT = BASE["w_v", 0], BASE["w_u", 0], BASE["w_out", 0]
        ACT_EVACS = 32
        ACT_PER_LAYER = 16 + EXP_TILES

        @block.sync
        def _(sp):
            def load(src, base, i, s, first=False):
                if not first:
                    sp.wait_ge(s_l0, 4 * i + (base + s - 3))
                    sp.wait_ge(s_l1, 4 * i + (base + s - 3))
                tile = src[s] if first else src[ds(4 * i + s, 1)]
                sp.dma_start(raw[s % RAW][:, :], tile).then_inc(s_raw[s % RAW], 16)

            def load_ada(m, s, first=False):
                if not first:
                    sp.wait_ge(s_acc, m - 3)
                sp.dma_start(ada[s][:, :], ada_d[m] if isinstance(m, int) else ada_d[ds(m, 1)]).then_inc(s_ada[s], 16)

            def load_ada_v(m, s):
                sp.wait_ge(s_acc, m - 3)
                sp.dma_start(ada_v[s][:, :], ada_d[ds(m, 1)]).then_inc(s_ada[s], 16)

            for dst, src in first_loads:
                sp.dma_start(dst, src).then_inc(s_first, 16)
            for s in range(4):
                load_ada(s, s, first=True)
            sp.dma_start(XT[:, :, :], xt_d).then_inc(s_x, 16)
            with sp.Fori(1, ADA_FRONT // 4) as i:
                for s in range(4):
                    load_ada(4 * i + s, s)
            for s in range(RAW):
                load(stream_dram["w_v", 0], 0, 0, s, first=True)
            for s in range(4):
                load_ada(ADA_FRONT + s, s)
            for dst, src in small_loads:
                sp.dma_start(dst, src).then_inc(s_small, 16)
            with sp.Fori(1, 16 // 4) as i:
                for s in range(4):
                    load(stream_dram["w_v", 0], 0, i, s)
                    load_ada(4 * i + (ADA_FRONT + s), s)
            with sp.Fori(0, (ADA_MLP - 16) // 4) as i:
                for s in range(4):
                    load(stream_dram["w_u", 0], W_U, i, s)
                    load_ada(4 * i + (ADA_FRONT + 16 + s), s)
            with sp.Fori((ADA_MLP - 16) // 4, 16 // 4) as i:
                for s in range(4):
                    load(stream_dram["w_u", 0], W_U, i, s)
            sp.dma_start(keys[:, 0], k1_d[0]).then_inc(s_keys, 16)
            sp.dma_start(keys[:, 1], k2_d[0]).then_inc(s_keys, 16)
            for name, layer, tiles in STREAM[2:]:
                src, base = stream_dram[name, layer], BASE[name, layer]
                done = 0
                for lo, hi, chunk in ADA_SPANS if (name, layer) == ("v", 0) else ():
                    with sp.Fori(done // 4, lo // 4) as i:
                        for s in range(4):
                            load(src, base, i, s)
                    with sp.Fori(chunk, chunk + (hi - lo) // 12) as x:
                        for s in range(12):
                            load(src, base, 3 * x + (lo // 4 - 3 * chunk), s)
                            if s in ADA_SLOTS:
                                k = ADA_SLOTS.index(s)
                                load_ada_v(KT * x + (ADA_FRONT + ADA_MLP + k), k % 4)
                    done = hi
                with sp.Fori(done // 4, tiles // 4) as i:
                    for s in range(4):
                        load(src, base, i, s)
            for p in range(4):
                sp.wait_ge(s_hf, 4 * (NORMS - 1) + p + 1)
                sp.dma_start(out_d[:, 2 * p:2 * p + 2, :], hf[:, 2 * p:2 * p + 2, :]).then_inc(s_out, 16)
            sp.wait_ge(s_out, 64)

        @block.gpsimd
        def _(pool):
            pool.memset(ident[:, :], 0.0).then_inc(s_const, 1)
            pool.memset(mean_w[:, :], 1.0 / D).then_inc(s_const, 1)
            pool.memset(eps[:, :], EPS).then_inc(s_const, 1)
            pool.memset(ones[:, :], 1.0).then_inc(s_const, 1)
            pool.iota(iota[:, :], [[1, KEYS]], base=0, channel_multiplier=0,
                      allow_small_or_imprecise_dtypes=True).then_inc(s_const, 1)
            pool.wait_ge(s_const, 5)
            pool.affine_select(out=ident[:, :], in_=ident[:, :], compare_op=ALU.not_equal, fill=1.0, base=0,
                               pattern=[[-1, P]], channel_multiplier=1).then_inc(s_const, 1)

            def low_second(base, i, s):
                slot = (2 * s + 1) % 4
                pool.wait_ge(s_h, 8 * i + (2 * (base + s) + 2))
                nc.gpsimd.tensor_tensor(wL[slot][:, :], raw[s % RAW][:, HALF:2 * HALF], wH[slot][:, :].bitcast(fp32),
                                        ALU.subtract).then_inc(s_l1, 1)

            def low_gated(layer, i, s):
                pool.wait_ge(s_gH2, 4 * i + (layer * EXP_TILES + s + 1))
                pool.wait_ge(s_const, 6)
                nc.gpsimd.tensor_tensor(gateL[s % 2][:, :], R[:, ds(4 * i + s, 1), :].rearrange("p a t -> p (a t)"),
                                        gateH[s % 2][:, :].bitcast(fp32), ALU.subtract).then_inc(s_gL2, 1)

            low_second(0, 0, 0)
            low_second(0, 0, 1)
            for layer in range(LAYERS):
                start, v = (0, BASE["p_in", 1])[layer], BASE["v", layer]
                with pool.Fori(start // 4, v // 4) as i:
                    for s in range(4):
                        low_second(0, i, s + 2)
                low_gated(layer, 0, 0)
                low_gated(layer, 0, 1)
                for lo, hi in ((0, 29), (29, 30), (30, 31)):
                    with pool.Fori(lo, hi) as i:
                        for s in range(4):
                            low_gated(layer, i, s + 2)
                            low_second(v, i, s + 2)
                    if layer == 0 and lo == 0:
                        pool.wait_ge(s_acc, ADA_FRONT + ADA_MLP + ADA_V)
                        pool.dma_start(UV[:, 0:8, :], p_grp_d).then_inc(s_late, 16)
                    if layer == 0 and lo == 29:
                        pool.dma_start(keys[:, 0], k1_d[1]).then_inc(s_late, 16)
                        pool.dma_start(keys[:, 1], k2_d[1]).then_inc(s_late, 16)
                for s in range(4):
                    if s < 2:
                        low_gated(layer, 31, s + 2)
                    if layer < LAYERS - 1 or s < 2:
                        low_second(v, 31, s + 2)

        @block.scalar
        def _(act):
            def split_high(base, i, s, halves=(0, 1)):
                for half in halves:
                    q = 8 * i + (2 * (base + s) + half)
                    if half == 0:
                        act.wait_ge(s_raw[s % RAW], 16 * i + (base + s) // 4 * 16 + 16)
                    if not (isinstance(q, int) and q < 4):
                        act.wait_ge(s_pe, q - 3)
                    nc.scalar.activation(wH[(2 * s + half) % 4][:, :], raw[s % RAW][:, half * HALF:half * HALF + HALF],
                                         ACT.Copy).then_inc(s_h, 1)

            def ahead(base, i, s):
                split_high(base, i, s + 2)

            def square(j):
                return nc.scalar.activation(sq[:, j, :], XT[:, j, :], ACT.Square).then_inc(s_sq, 1)

            def root(n):
                act.wait_ge(s_ms, n + 1)
                nc.scalar.activation(std[:, :], O[0][:, 0:T], ACT.Sqrt, bias=eps[:, :]).then_inc(s_std, 1)

            def norm(n):
                if n > 0:
                    root(n)
                else:
                    act.wait_ge(s_mod, 1)
                for p in range(4):
                    act.wait_ge(s_xn, 4 * n + p + 1)
                    for k in (2 * p, 2 * p + 1):
                        if n == NORMS - 1:
                            ins = nc.scalar.activation(hf[:, k, :], sq[:, k, :], ACT.Copy, scale=fg[:, k:k + 1])
                        else:
                            ins = nc.scalar.activation(hf[:, k, :], sq[:, k, :], ACT.Identity,
                                                       bias=modcol(n // 2, 3 * (n % 2), k, 1), scale=gs[:, n, k:k + 1])
                    ins.then_inc(s_hf, 1)
                    if n < NORMS - 1:
                        act.wait_ge(s_hf, 4 * n + p + 1)
                        nc.scalar.activation(hH[:, 2 * p:2 * p + 2, :], hf[:, 2 * p:2 * p + 2, :], ACT.Copy)\
                            .then_inc(s_hH, 1)

            def gated_high(f, count):
                act.wait_ge(s_gf, count)
                nc.scalar.activation(gH[:, f, :], UV[:, SGU_FT + f, :], ACT.Copy).then_inc(s_gH, 1)

            def warm():
                nc.scalar.activation(tick[:, 6:7], eps[:, :], ACT.Gelu)

            act.wait_ge(s_first, FIRST)
            nc.scalar.activation(csT[:, :], csT[:, :], ACT.Silu).then_inc(s_silu, 1)
            act.wait_ge(s_x, 16)
            for j in range(KT):
                square(j)
            act.wait_ge(s_const, 6)
            root(0)
            split_high(0, 0, 0)
            split_high(0, 0, 1)
            norm(0)
            for layer in range(LAYERS):
                if layer == 0:
                    warm()
                    with act.Fori(0, 16 // 4) as i:
                        for s in range(4):
                            ahead(W_V, i, s)
                            nc.scalar.activation(UV[:, ds(4 * i + (SGU_FT + s), 1), :], ring[s][:, 0:T], ACT.Gelu)\
                                .then_inc(s_bank_a, 1)
                    for t in range(16):
                        ahead(W_U, t // 4, t % 4)
                        nc.scalar.activation(UV[:, t, :], ring[t % 4][:, 0:T], ACT.Gelu).then_inc(s_bank_a, 1)
                        if t < 8:
                            c, f = t // 4, t % 4
                            act.wait_ge(s_vt, t + 1)
                            nc.scalar.activation(vtok[:, c, f * 512:f * 512 + 512], O[f][:, :], ACT.Copy)
                            nc.scalar.activation((sq, hf)[c][:, 2 * f:2 * f + 2, :].rearrange("p a b -> p (a b)"), O[f][:, :], ACT.Square,
                                                 accum_out=ssq[:, t:t + 1]).then_inc(s_vc, 1)
                        if t == 8:
                            act.wait_ge(s_ssq, 1)
                            nc.scalar.activation(vstd[:, :], ssum[:, :], ACT.Sqrt, bias=eps[:, :], scale=1.0 / SGU_W)\
                                .then_inc(s_vstd, 1)
                        if t > 10:
                            for f in (2 * (t - 11), 2 * (t - 11) + 1):
                                gated_high(f, f + 1)
                    for f in range(10, SGU_FT):
                        gated_high(f, f + 1)
                    act.wait_ge(s_small, SMALL)
                    for j in range(KT):
                        for kk in range(2):
                            ahead(W_OUT, j // 2, 2 * (j % 2) + kk)
                        if j:
                            act.wait_ge(s_bank_v, 4 + j)
                            square(j - 1)
                    act.wait_ge(s_bank_v, 4 + KT)
                    square(KT - 1)
                else:
                    base = BASE["p_in", 1]
                    for j in range(KT):
                        ahead(base, j // 4, j % 4)
                    for f in range(KT):
                        gated_high(f, SGU_FT + f + 1)
                    base = BASE["p_out", 1]
                    for j in range(KT):
                        ahead(base, j // 4, j % 4)
                        if j:
                            act.wait_ge(s_bank_v, 4 + 16 + j)
                            square(j - 1)
                    act.wait_ge(s_bank_v, 4 + 16 + KT)
                    square(KT - 1)
                norm(2 * layer + 1)
                with act.Fori(0, 16 // 4) as i:
                    for s in range(4):
                        ahead(BASE["w_q", layer], i, s)
                        nc.scalar.activation(UV[:, ds(4 * i + s, 1), :], ring[s][:, 0:T], ACT.Copy)\
                            .then_inc(s_bank_a, 1)

                def experts(lo, hi):
                    with act.Fori(lo // 4, hi // 4) as i:
                        for s in range(4):
                            ahead(BASE["u", layer], i, s)
                            nc.scalar.activation(R[:, ds(4 * i + s, 1), :], ring[s][:, 0:T], ACT.Gelu)\
                                .then_inc(s_bank_a, 1)

                warm()
                experts(0, 52)
                act.wait_ge(s_diff, layer + 1)
                nc.scalar.activation(best[:, :, :, :], ex[:, :, :, :], ACT.Exp).then_inc(s_exp, 1)
                warm()
                experts(52, 80)
                act.wait_ge(s_sel, layer + 1)
                experts(80, 128)

                act.wait_ge(s_gated, NGRP * (2 * layer + 1))

                def split_gated(i, s):
                    nc.scalar.activation(gateH[s % 2][:, :], R[:, ds(4 * i + s, 1), :].rearrange("p a t -> p (a t)"),
                                         ACT.Copy).then_inc(s_gH2, 1)

                def ahead_gated(i, s, band2=False):
                    base = BASE["v", layer]
                    split_high(base, i, s + 2, (0,))
                    if band2:
                        act.wait_ge(s_gated, NGRP * (2 * layer + 2))
                    act.wait_ge(s_pe, 8 * i + 2 * (base + s + 1))
                    act.wait_ge(s_const, 6)
                    split_gated(i, s + 2)
                    split_high(base, i, s + 2, (1,))

                split_gated(0, 0)
                split_gated(0, 1)
                last = BAND // 4 - 1
                with act.Fori(0, last) as i:
                    for s in range(4):
                        ahead_gated(i, s)
                for s in range(4):
                    ahead_gated(last, s, band2=(s == 2))
                with act.Fori(last + 1, 31) as i:
                    for s in range(4):
                        ahead_gated(i, s)
                for s in range(4):
                    if s < 2:
                        ahead_gated(31, s)
                    elif layer < LAYERS - 1:
                        ahead(BASE["v", layer], 31, s)
                act.wait_ge(s_pe, 2 * (BASE["v", layer] + EXP_TILES) - 1)
                for tt in range(TT):
                    nc.scalar.activation(otok[:, tt, 0:512], O[2 * tt][:, :], ACT.Copy).then_inc(s_oc_a, 1)
                for j in range(KT):
                    act.wait_ge(s_res, KT * layer + j + 1)
                    square(j)
                norm(2 * layer + 2)

        @block.vector
        def _(dve):
            steps = [0]

            def step(ins):
                steps[0] += 1
                ins.then_inc(s_vstep, 1)
                return steps[0]

            def after(n):
                dve.wait_ge(s_vstep, n)

            def low_first(base, i, s):
                dve.wait_ge(s_h, 8 * i + (2 * (base + s) + 1))
                nc.vector.tensor_tensor(wL[(2 * s) % 4][:, :], raw[s % RAW][:, 0:HALF],
                                        wH[(2 * s) % 4][:, :].bitcast(fp32), ALU.subtract).then_inc(s_l0, 1)

            def ahead(base, i, s):
                low_first(base, i, s + 2)

            def ada_tile(m, s, turn, chunk, k):
                dve.wait_ge(s_ada[s], 16 * turn)
                a, t, w = acc[:, chunk, :], ada[s][:, :], csT[:, k:k + 1]
                if k == 0:
                    nc.vector.tensor_scalar(a, t, w, None, ALU.mult).then_inc(s_acc, 1)
                else:
                    dve.wait_ge(s_acc, m)
                    nc.vector.scalar_tensor_tensor(a, t, w, a, ALU.mult, ALU.add).then_inc(s_acc, 1)

            def ada_tile_v(x, k):
                dve.wait_ge(s_ada[k % 4], 32 * x + 16 * ((ADA_FRONT + ADA_MLP) // 4 + k // 4 + 1))
                a, t, w = acc_v[:, ds(x, 1), :].rearrange("p a d -> p (a d)"), ada_v[k % 4][:, :], csT[:, k:k + 1]
                if k == 0:
                    nc.vector.tensor_scalar(a, t, w, None, ALU.mult).then_inc(s_acc, 1)
                else:
                    dve.wait_ge(s_acc, KT * x + (ADA_FRONT + ADA_MLP + k))
                    nc.vector.scalar_tensor_tensor(a, t, w, a, ALU.mult, ALU.add).then_inc(s_acc, 1)

            def split_sums(x, sums, parts, stages=(0, 1)):
                if 0 in stages:
                    after(step(nc.vector.tensor_copy(parts[:, x, 0, :], sums[:, x, :])))
                    step(nc.vector.tensor_tensor(sums[:, x, :], sums[:, x, :], parts[:, x, 0, :], ALU.subtract))
                if 1 in stages:
                    after(steps[0])
                    after(step(nc.vector.tensor_copy(parts[:, x, 1, :], sums[:, x, :])))
                    nc.vector.tensor_tensor(parts[:, x, 2, :], sums[:, x, :], parts[:, x, 1, :], ALU.subtract)\
                        .then_inc(s_acc2, 1)

            def modulations(n, chunks, bank, norms):
                lo, hi = chunks[0] * KT, (chunks[-1] + 1) * KT
                dve.wait_ge(s_modp, n)
                last = step(nc.vector.tensor_tensor(mod[:, lo:hi], bank[:, 0:hi - lo], adab[:, lo:hi], ALU.add))
                after(last)
                for m in norms:
                    gain = (n1, n2)[m % 2]
                    last = step(nc.vector.scalar_tensor_tensor(gs[:, m, :], modcol(m // 2, 3 * (m % 2) + 1), 1.0,
                                                               gain[:, m // 2 * KT:m // 2 * KT + KT], ALU.add, ALU.mult))
                after(last)
                nc.vector.memset(tick[:, 0:1], 0.0).then_inc(s_mod, 1)

            def norm(n):
                dve.wait_ge(s_std, n + 1)
                after(step(nc.vector.reciprocal(rstd[:, :], std[:, :])))

                def scaled(p):
                    nc.vector.tensor_tensor(sq[:, 2 * p:2 * p + 2, :], XT[:, 2 * p:2 * p + 2, :],
                                            rstd[:, None, :].to_broadcast([P, 2, T]), ALU.mult).then_inc(s_xn, 1)

                def low(p):
                    dve.wait_ge(s_hH, 4 * n + p + 1)
                    nc.vector.tensor_tensor(hL[:, 2 * p:2 * p + 2, :], hf[:, 2 * p:2 * p + 2, :],
                                            hH[:, 2 * p:2 * p + 2, :].bitcast(fp32), ALU.subtract).then_inc(s_hin, 1)

                scaled(0)
                scaled(1)
                if n == NORMS - 1:
                    scaled(2)
                    scaled(3)
                else:
                    if n == 0:
                        for m in range(ADA_EARLY, ADA_FRONT):
                            ada_tile(m, m % 4, m // 4 + 1, m // KT, m % KT)
                        low_first(0, 0, 0)
                        low_first(0, 0, 1)
                        modulations(2, (0, 1), ring[0], (0,))
                    low(0)
                    scaled(2)
                    low(1)
                    scaled(3)
                    low(2)
                    low(3)

            def residual(layer, chunk, j, bank, half=0):
                return nc.vector.scalar_tensor_tensor(XT[:, j, :], bank[:, half * T:half * T + T],
                                                      modcol(layer, chunk, j, 1), XT[:, j, :], ALU.mult, ALU.add)

            dve.wait_ge(s_const, 6)
            nc.vector.tensor_copy(ones_b[:, :], ones[:, :])
            nc.vector.tensor_copy(iota_g[:, :, :], iota[:, :, None].to_broadcast([P, KEYS, GRP]))
            def window_ready(g):
                place, hi_t, lo_t = UV[:, 12, :], UV[:, 13, :], UV[:, 14, :]
                if g == PG - 1:
                    step(nc.vector.memset(Z[:, :, 0:PAD], 0.0))
                    step(nc.vector.memset(Z[:, :, PAD + T:], 0.0))
                    step(nc.vector.tensor_scalar(UV[:, 12, 0:P], iota[:, :], 0.0, None, ALU.add))
                    after(step(nc.vector.tensor_scalar(UV[:, 12, P:T], iota[:, :], float(P), None, ALU.add)))
                half = float(1 << g)
                after(steps[0])
                step(nc.vector.tensor_scalar(hi_t, place, half, float(T), ALU.add, ALU.min))
                after(step(nc.vector.tensor_scalar(lo_t, place, -half, 0.0, ALU.add, ALU.max)))
                after(step(nc.vector.tensor_tensor(hi_t, hi_t, lo_t, ALU.subtract)))
                step(nc.vector.reciprocal(UV[:, 8 + g, :], hi_t))

            nc.vector.memset(tick[:, 1:2], 0.0).then_inc(s_bank_v, 4)
            nc.vector.memset(tick[:, 2:3], 0.0).then_inc(s_bank_a, 4)
            dve.wait_ge(s_first, FIRST)
            dve.wait_ge(s_silu, 1)
            for m in range(ADA_EARLY):
                ada_tile(m, m % 4, m // 4 + 1, m // KT, m % KT)
            dve.wait_ge(s_x, 16)
            norm(0)
            for layer in range(LAYERS):
                if layer == 0:
                    for t in range(16):
                        ahead(W_V, t // 4, t % 4)
                        m = ADA_FRONT + t
                        ada_tile(m, m % 4, m // 4 + 1, t // KT, t % KT)

                    def gate_tile(f):
                        dve.wait_ge(s_mixed, f + 1)
                        g = f // (SGU_FT // SGU_G)
                        nc.vector.scalar_tensor_tensor(
                            hf[:, f % 8, :].rearrange("p (c t) -> p c t", c=TT),
                            O[f % 4][:, 0:T].rearrange("p (c t) -> p c t", c=TT), vg[:, f:f + 1],
                            bs[:, g:g + 1, :].to_broadcast([P, TT, P]), ALU.mult, ALU.add).then_inc(s_sv, 1)

                    def gate_by(f):
                        dve.wait_ge(s_sv, f + 1)
                        dve.wait_ge(s_bank_a, 4 + SGU_FT + f + 1)
                        nc.vector.tensor_tensor(UV[:, SGU_FT + f, :], hf[:, f % 8, :], UV[:, f, :], ALU.mult)\
                            .then_inc(s_gf, 1)

                    def gated_low(f):
                        dve.wait_ge(s_gH, f + 1)
                        nc.vector.tensor_tensor(gL[:, f, :], UV[:, SGU_FT + f, :], gH[:, f, :].bitcast(fp32),
                                                ALU.subtract).then_inc(s_gL, 1)

                    for t in range(16):
                        ahead(W_U, t // 4, t % 4)
                        if t < ADA_MLP - 16:
                            m = ADA_FRONT + 16 + t
                            ada_tile(m, m % 4, m // 4 + 1, 2, t)
                        if t == 7:
                            dve.wait_ge(s_vc, 8)
                            nc.vector.tensor_reduce(ssum[:, :], ssq[:, :].rearrange("p (c f) -> p c f", c=TT), AX.X,
                                                    ALU.add).then_inc(s_ssq, 1)
                        if t == 8:
                            dve.wait_ge(s_vstd, 1)
                            after(step(nc.vector.reciprocal(ssum[:, :], vstd[:, :])))
                            for c in range(TT):
                                nc.vector.tensor_scalar(vtok[:, c, :], vtok[:, c, :], ssum[:, c:c + 1], None, ALU.mult)\
                                    .then_inc(s_vn, 1)
                        if t < 4:
                            dve.wait_ge(s_acc, ADA_FRONT + 16)
                            split_sums(t // 2, acc, parts_m, (t % 2,))
                        if t == 10:
                            dve.wait_ge(s_small, SMALL)
                            modulations(4, (2, 3, 4), O[3], (1,))
                        if t > 9:
                            f = 2 * (t - 10)
                            gate_tile(f)
                            gate_tile(f + 1)
                            gate_by(f)
                            gate_by(f + 1)
                        if t > 11:
                            gated_low(2 * (t - 12))
                            gated_low(2 * (t - 12) + 1)
                    for f in range(12, SGU_FT):
                        gate_tile(f)
                        gate_by(f)
                        gated_low(f - 4)
                    for f in range(12, SGU_FT):
                        gated_low(f)
                    for j in range(KT):
                        for s in range(2):
                            ahead(W_OUT, j // 2, 2 * (j % 2) + s)
                        dve.wait_ge(s_pe, 2 * (W_OUT + 4 * (j // 2) + 3 + j % 2))
                        residual(0, 2, j, ring[j % 4]).then_inc(s_bank_v, 1)
                else:
                    base = BASE["p_in", 1]
                    W = PAD + T + PAD
                    lev = [hf[:, :, :].rearrange("p a b -> p (a b)")[:, a * 2 * W:(a + 1) * 2 * W]
                           .rearrange("p (c w) -> p c w", c=2) for a in range(2)]
                    def pooled_full(n):
                        dve.wait_ge(s_pg, n + 1)
                        nc.vector.tensor_scalar(UV[:, SGU_FT + n, :], pool_bank(n)[:, 0:T],
                                                ps[:, POOL_ORDER[n]:POOL_ORDER[n] + 1], None, ALU.mult).then_inc(s_gf, 1)

                    def pooled_low(n):
                        dve.wait_ge(s_gH, SGU_FT + n + 1)
                        nc.vector.tensor_tensor(gL[:, n, :], UV[:, SGU_FT + n, :], gH[:, n, :].bitcast(fp32),
                                                ALU.subtract).then_inc(s_gL, 1)

                    for j in range(KT):
                        ahead(base, j // 4, j % 4)
                        if j in (0, 2):
                            window_ready(1 - j // 2)
                        f = POOL_ORDER[j]
                        g = f // 2
                        dve.wait_ge(s_pe, 2 * (base + j + 1))
                        nc.vector.tensor_copy(Z[:, f, PAD:PAD + T], ring[j % 4][:, 0:T]).then_inc(s_bank_v, 1)
                        if j % 2 == 0:
                            continue
                        dve.wait_ge(s_bank_v, 4 + KT + j + 1)
                        z2 = Z[:, 2 * g:2 * g + 2, :]
                        after(step(nc.vector.tensor_tensor(lev[0][:, :, 1:W - 1], z2[:, :, 0:W - 2], z2[:, :, 1:W - 1],
                                                           ALU.add)))
                        lo, hi, cur = 1, W - 1, 0
                        for m in range(1, g + 1):
                            r = 1 << (m - 1)
                            lo, hi = lo + r, hi - r
                            after(step(nc.vector.tensor_tensor(lev[1 - cur][:, :, lo:hi], lev[cur][:, :, lo - r:hi - r],
                                                               lev[cur][:, :, lo + r:hi + r], ALU.add)))
                            cur = 1 - cur
                        pooled = vtok[:, 0, 2 * g * T:(2 * g + 2) * T].rearrange("p (c t) -> p c t", c=2)
                        after(steps[0])
                        after(step(nc.vector.tensor_tensor(pooled, lev[cur][:, :, PAD:PAD + T],
                                                           UV[:, 8 + g:9 + g, :].to_broadcast([P, 2, T]), ALU.mult)))
                        nc.vector.tensor_tensor(pooled, pooled, z2[:, :, PAD:PAD + T], ALU.subtract).then_inc(s_pooled, 1)
                        if j > 4:
                            pooled_full(j - 5)
                            pooled_full(j - 4)
                        if j > 6:
                            pooled_low(0)
                            pooled_low(1)
                    for n in range(4, KT):
                        pooled_full(n)
                        pooled_low(n - 2)
                    pooled_low(KT - 2)
                    pooled_low(KT - 1)
                    base = BASE["p_out", 1]
                    for j in range(KT):
                        ahead(base, j // 4, j % 4)
                        dve.wait_ge(s_pe, 2 * (base + j + 1))
                        residual(1, 2, j, ring[j % 4]).then_inc(s_bank_v, 1)
                norm(2 * layer + 1)

                def top16(values, out_v, out_i):
                    after(step(nc.vector.max(out_v[:, 0:8], values)))
                    a = step(nc.vector.max_index(out_i[:, 0:8], out_v[:, 0:8], values))
                    after(a)
                    after(step(nc.vector.match_replace(values, out_v[:, 0:8], values, -3.0e38)))
                    after(step(nc.vector.max(out_v[:, 8:16], values)))
                    return step(nc.vector.max_index(out_i[:, 8:16], out_v[:, 8:16], values))

                def fetch_scores(b):
                    for tt in range(TT):
                        dve.wait_ge(s_sc, 8 * layer + 2 * b + tt + 1)
                        nc.vector.tensor_copy(S[:, tt, 4 * b:4 * b + 4, :],
                                              score_bank(b, tt)[:, :].rearrange("p (a n) -> p a n", a=4))\
                            .then_inc(s_scc, 1)
                    dve.wait_ge(s_scc, 8 * layer + 2 * b + 2)

                def best_keys(m):
                    tt, j = m // 4 % 2, m // 8 * 4 + m % 4
                    top16(S[:, tt, j, :], top_v[:, tt, j, :], top_i[:, tt, j, :])

                for t in range(16):
                    ahead(BASE["w_q", layer], t // 4, t % 4)
                    if t % 4 == 2 and t > 4:
                        fetch_scores(t // 4 - 1)
                    if t > 6:
                        best_keys(t - 7)

                def topk_step(n):
                    if n == 0:
                        fetch_scores(3)
                    if n < 23:
                        best_keys(n + 9)
                    elif n < 39:
                        tt, h = (n - 23) // 8, (n - 23) % 8
                        if h == 0:
                            after(steps[0])
                            v = top_v[:, tt, :, :].rearrange("p (h s) k -> p h s k", s=2)
                            after(step(nc.vector.tensor_tensor(
                                C[:, :, :].rearrange("p h (a b) -> p h a b", a=TOPK),
                                v[:, :, 0, :, None].to_broadcast([P, HEADS, TOPK, TOPK]),
                                v[:, :, 1, None, :].to_broadcast([P, HEADS, TOPK, TOPK]), ALU.add)))
                        top16(C[:, h, :], best[:, tt, h, :], pos[:, tt, h, :])
                    elif n == 39:
                        after(steps[0])
                        flat = pos[:, :, :, :].rearrange("p t h k -> p t (h k)")
                        step(nc.vector.tensor_scalar(pos_ab[:, 0], flat, 4, None, ALU.logical_shift_right))
                        step(nc.vector.tensor_scalar(pos_ab[:, 1], flat, 15, None, ALU.bitwise_and))
                        b = best[:, :, :, :].rearrange("p t h k -> p (t h) k")
                        nc.vector.tensor_tensor(ex[:, :, :, :].rearrange("p t h k -> p (t h) k"), b,
                                                b[:, :, 0:1].to_broadcast([P, TT * HEADS, TOPK]),
                                                ALU.subtract).then_inc(s_diff, 1)
                        after(steps[0])
                    elif n == 40:
                        step(nc.vector.tensor_copy(ab[:, :, :, :], pos_ab[:, :, :, :]))
                        step(nc.vector.tensor_copy(top_f[:, :, :, :], top_i[:, :, :, :]))
                        after(steps[0])
                    elif n < 57:
                        tt, side, hh, odd = (n - 41) // 8, (n - 41) // 4 % 2, (n - 41) // 2 % 2, (n - 41) % 2
                        half = HK // 2
                        if not odd:
                            after(step(nc.vector.tensor_tensor(
                                M[:, :, :], ab[:, side, tt, hh * half:hh * half + half, None].to_broadcast([P, half, TOPK]),
                                iota[:, None, 0:TOPK].to_broadcast([P, half, TOPK]), ALU.is_equal)))
                            keys_of = top_f[:, tt, :, :].rearrange("p (h s) k -> p h s k", s=2)[:, 4 * hh:4 * hh + 4, side, None, :]
                            m4 = M[:, :, :].rearrange("p (h k) a -> p h k a", h=4)
                            after(step(nc.vector.tensor_tensor(m4, m4, keys_of.to_broadcast([P, 4, TOPK, TOPK]), ALU.mult)))
                        else:
                            after(step(nc.vector.tensor_reduce(sel[:, side, tt, hh * half:hh * half + half], M[:, :, :],
                                                               AX.X, ALU.add)))
                    else:
                        dve.wait_ge(s_exp, layer + 1)
                        b = best[:, :, :, :].rearrange("p t h k -> p (t h) k")
                        after(step(nc.vector.tensor_reduce(zsum[:, :], b, AX.X, ALU.add)))
                        after(step(nc.vector.reciprocal(zsum[:, :], zsum[:, :])))
                        nc.vector.tensor_tensor(sel[:, 2, :, :].rearrange("p t (h k) -> p (t h) k", h=HEADS), b,
                                                zsum[:, :, None].to_broadcast([P, TT * HEADS, TOPK]), ALU.mult)\
                            .then_inc(s_sel, 1)

                def token_row(i, x, row, n):
                    at = selT[:, row, ds(2 * GRP * i + GRP * x, GRP)]
                    return at[:, None, :].to_broadcast([P, n, GRP]) if isinstance(row, int) else \
                        at[:, :, None, :].to_broadcast([P, 3, n, GRP])

                def one_hot(i, x, band, first=False):
                    nc.vector.tensor_tensor(oneB[x][:, :, :], iota_g[:, :, :], token_row(i, x, 1, KEYS), ALU.is_equal)
                    if layer or band or x or not first:
                        dve.wait_ge(s_one, 2 * i + ((2 * layer + band) * NGRP + x))
                    nc.vector.tensor_tensor(oneE[:, :, :], iota_g[:, band * BAND:(band + 1) * BAND, :],
                                            token_row(i, x, 0, BAND), ALU.is_equal).then_inc(s_eq, 1)

                def times_gates(i, x, band):
                    dve.wait_ge(s_eq, 2 * i + ((2 * layer + band) * NGRP + x + 1))
                    nc.vector.tensor_tensor(oneA[x][:, :, :, :], oneE[:, None, :, :].to_broadcast([P, 3, BAND, GRP]),
                                            token_row(i, x, slice(2, 5), BAND), ALU.mult).then_inc(s_one, 1)

                def multiply(i, x, band):
                    dve.wait_ge(s_grid, 2 * i + ((2 * layer + band) * NGRP + x + 1))
                    r = R[:, band * BAND:(band + 1) * BAND, ds(2 * GRP * i + GRP * x, GRP)]
                    nc.vector.tensor_tensor(r, (O, ring)[band][x][:, :].rearrange("p (t n) -> p n t", t=GRP), r,
                                            ALU.mult).then_inc(s_gated, 1)

                def gate_step(i, s, band, first=False, last=False):
                    if s == 0:
                        one_hot(i, 0, band, first)
                        if last:
                            times_gates(i, 0, band)
                    if s == 1:
                        if not last:
                            times_gates(i, 0, band)
                        if not first:
                            multiply(i - 1, 1, band)
                        if last:
                            one_hot(i, 1, band)
                            times_gates(i, 1, band)
                    if s == 2:
                        if last:
                            multiply(i, 0, band)
                            multiply(i, 1, band)
                        else:
                            one_hot(i, 1, band)
                    if s == 3 and not last:
                        times_gates(i, 1, band)
                        multiply(i, 0, band)

                base = BASE["u", layer]
                for n in range(BAND):
                    ahead(base, n // 4, n % 4)
                    if n < 58:
                        topk_step(n)
                    if n == 62:
                        dve.wait_ge(s_selT, layer + 1)
                        for a in range(3):
                            n = step(nc.vector.tensor_copy(selT[:, a, :], O[a][:, 0:T]))
                        after(n)
                        after(step(nc.vector.tensor_tensor(gate_rest[:, :], O[2][:, 0:T], selT[:, 2, :], ALU.subtract)))
                        after(step(nc.vector.tensor_copy(selT[:, 3, :], gate_rest[:, :])))
                        after(step(nc.vector.tensor_tensor(selT[:, 4, :], gate_rest[:, :], selT[:, 3, :], ALU.subtract)))
                dve.wait_ge(s_bank_a, 4 + ACT_EVACS + ACT_PER_LAYER * layer + 16 + BAND)
                for s in range(4):
                    ahead(base + BAND, 0, s)
                    gate_step(0, s, 0, first=True)
                with dve.Fori(1, PAIRS - 1) as i:
                    for s in range(4):
                        ahead(base + BAND, i, s)
                        gate_step(i, s, 0)
                for s in range(4):
                    ahead(base + BAND, PAIRS - 1, s)
                    gate_step(PAIRS - 1, s, 0, last=True)

                base = BASE["v", layer]
                dve.wait_ge(s_bank_a, 4 + ACT_EVACS + ACT_PER_LAYER * (layer + 1))
                for s in range(4):
                    ahead(base, 0, s)
                    gate_step(0, s, 1, first=True)
                def beside_ada(lo, hi, chunk):
                    with dve.Fori(chunk, chunk + (hi - lo) // 12) as x:
                        for s in range(12):
                            i = 3 * x + (lo // 4 - 3 * chunk + s // 4)
                            ahead(base, i, s % 4)
                            if hi < BAND:
                                gate_step(i, s % 4, 1)
                            if s in ADA_SLOTS:
                                ada_tile_v(x, ADA_SLOTS.index(s))

                if layer == 0:
                    (lo, hi, chunk), (lo2, hi2, chunk2) = ADA_SPANS
                    with dve.Fori(1, lo // 4) as i:
                        for s in range(4):
                            ahead(base, i, s)
                            gate_step(i, s, 1)
                    beside_ada(lo, hi, chunk)
                else:
                    with dve.Fori(1, PAIRS - 1) as i:
                        for s in range(4):
                            ahead(base, i, s)
                            gate_step(i, s, 1)
                for s in range(4):
                    ahead(base, PAIRS - 1, s)
                    gate_step(PAIRS - 1, s, 1, last=True)
                if layer == 0:
                    beside_ada(lo2, hi2, chunk2)
                if layer == 0:
                    dve.wait_ge(s_acc, ADA_FRONT + ADA_MLP + ADA_V)
                    for n in range(hi2, EXP_TILES):
                        ahead(base, n // 4, n % 4)
                        if n - hi2 < 14:
                            split_sums((n - hi2) // 2, acc_v, parts_v, ((n - hi2) % 2,))
                        if n == EXP_TILES - 1:
                            modulations(5, tuple(range(5, 12)), ring[3], (2, 3))
                        if n == EXP_TILES - 2:
                            window_ready(3)
                else:
                    with dve.Fori(BAND // 4, 31) as i:
                        for s in range(4):
                            ahead(base, i, s)
                    for s in range(2):
                        ahead(base, 31, s)
                dve.wait_ge(s_pe, 2 * (base + EXP_TILES))
                for tt in range(TT):
                    nc.vector.tensor_copy(otok[:, tt, 512:1024], O[2 * tt + 1][:, :]).then_inc(s_oc_v, 1)
                for j in range(KT):
                    if j % 2 == 0:
                        dve.wait_ge(s_ot, layer * 4 + j // 2 + 1)
                    residual(layer, 5, j, ring[j // 2], j % 2).then_inc(s_res, 1)
                if layer == 0:
                    window_ready(2)
                norm(2 * layer + 2)

        @block.tensor
        def _(pe):
            mm = nc.tensor.matmul

            def tile_product(base, i, s, bank, xH, xL, k0=0, first=True, last=True, pairs=None):
                for half in range(2):
                    pe.wait_ge((s_l0, s_l1)[half], 4 * i + (base + s + 1))
                    slot = (2 * s + half) % 4
                    for kk in range(4):
                        k = 4 * half + kk
                        if pairs and k % 2 == 0:
                            pe.wait_ge(pairs[0], pairs[1] + pairs[2] * (k // 2 + 1))
                        a, b = wH[slot][:, kk * P:kk * P + P], wL[slot][:, kk * P:kk * P + P]
                        mm(bank[:, 0:T], a, xH[:, k0 + k, :], start=(first and k == 0), stop=False)
                        mm(bank[:, 0:T], a, xL[:, k0 + k, :], start=False, stop=False)
                        ins = mm(bank[:, 0:T], b, xH[:, k0 + k, :], start=False, stop=(last and k == KT - 1))
                    ins.then_inc(s_pe, 1)

            def stage(name, layer, emptied, before, lo=0, hi=None, norm_n=None):
                base = BASE[name, layer]
                tiles = {n: t for n, l, t in STREAM}[name]
                with pe.Fori(lo // 4, (tiles if hi is None else hi) // 4) as i:
                    for s in range(4):
                        pe.wait_ge(emptied, 4 * i + (before + s + 1))
                        tile_product(base, i, s, ring[s], hH, hL,
                                     pairs=(s_hin, 4 * norm_n, 1) if norm_n is not None and s == 0 else None)

            def mean(n, j):
                pe.wait_ge(s_sq, KT * n + j + 1)
                ins = mm(O[0][:, 0:T], mean_w[:, :], sq[:, j, :], start=(j == 0), stop=(j == KT - 1))
                if j == KT - 1:
                    ins.then_inc(s_ms, 1)

            def modulations(sums, lo, hi, summed, bank):
                pe.wait_ge(s_acc, summed)
                for x in range(lo, hi):
                    for j in range(KT):
                        at = KT * (x - lo) + j
                        ins = mm(bank[:, at:at + 1], sums[:, x, j * P:j * P + P], ones[:, :], start=True, stop=True)
                ins.then_inc(s_modp, 1)

            def split_modulations(parts, chunks, ready, bank):
                pe.wait_ge(s_acc2, ready)
                for x in range(chunks):
                    for j in range(KT):
                        at = KT * x + j
                        for part in range(3):
                            ins = mm(bank[:, at:at + 1], parts[:, x, part, j * P:j * P + P], ones_b[:, :],
                                     start=(part == 0), stop=(part == 2))
                ins.then_inc(s_modp, 1)

            def mix_tile(f):
                if f == 0:
                    pe.wait_ge(s_vn, TT)
                if f >= 4:
                    pe.wait_ge(s_sv, f - 3)
                for c in range(TT):
                    ins = mm(O[f % 4][:, c * P:c * P + P], vtok[:, c, f * P:f * P + P],
                             ws[:, f // (SGU_FT // SGU_G), :], start=True, stop=True)
                ins.then_inc(s_mixed, 1)

            def group_product(n):
                f = POOL_ORDER[n]
                pe.wait_ge(s_pooled, n // 2 + 1)
                if n >= 4:
                    pe.wait_ge(s_gf, SGU_FT + n - 3)
                wg = UV[:, 0:8, :].rearrange("p a b -> p (a b)")
                for kk in range(2):
                    at, k = (2 * f + kk) * P, f // 2 * 2 + kk
                    ins = mm(pool_bank(n)[:, 0:T], wg[:, at:at + P], vtok[:, 0, k * T:k * T + T],
                             start=(kk == 0), stop=(kk == 1))
                ins.then_inc(s_pg, 1)

            def scores(layer, j):
                pe.wait_ge(s_bank_a, 4 + ACT_EVACS + ACT_PER_LAYER * layer + j + 1)
                b = j // 4
                if b > 1 and j % 4 == 0:
                    pe.wait_ge(s_scc, 8 * layer + 2 * (b - 1))
                for tt in range(TT):
                    ins = mm(score_bank(b, tt)[:, j % 4 * P:j % 4 * P + P], UV[:, j, tt * P:tt * P + P],
                             keys[:, j % 2, j // 2, :], start=True, stop=True)
                    if j % 4 == 3:
                        ins.then_inc(s_sc, 1)

            pe.wait_ge(s_const, 6)
            for j in range(KT):
                mean(0, j)
            modulations(acc, 0, 1, KT, ring[0])
            modulations(acc, 1, 2, ADA_FRONT, ring[0][:, KT:])
            pe.wait_ge(s_mod, 1)
            for layer in range(LAYERS):
                if layer == 0:
                    stage("w_v", 0, s_bank_a, 0, norm_n=0)
                    for t in range(16):
                        pe.wait_ge(s_bank_a, 16 + t + 1)
                        tile_product(W_U, t // 4, t % 4, ring[t % 4], hH, hL)
                        if t < 8:
                            c, f = t // 4, t % 4
                            if t == 0:
                                pe.wait_ge(s_bank_a, 4 + 16)
                            if t >= 4:
                                pe.wait_ge(s_vc, t - 3)
                            for q in range(4):
                                ins = nc.tensor.transpose(O[f][:, q * P:q * P + P],
                                                          UV[:, SGU_FT + 4 * f + q, c * P:c * P + P], ident[:, :])
                            ins.then_inc(s_vt, 1)
                        if t == 9:
                            pe.wait_ge(s_vc, 8)
                            split_modulations(parts_m, 2, 2, O[3])
                            modulations(acc, 2, 3, ADA_FRONT + ADA_MLP, O[3][:, 2 * KT:])
                        if t == 10:
                            pe.wait_ge(s_small, SMALL)
                        if t == 11:
                            pe.wait_ge(s_mod, 2)
                        if t > 9:
                            mix_tile(2 * (t - 10))
                            mix_tile(2 * (t - 10) + 1)
                    for f in range(12, SGU_FT):
                        mix_tile(f)
                    for t in range(2 * KT):
                        i, s = t // 4, t % 4
                        j, kk = 2 * i + s % 2, s // 2
                        if kk == 0:
                            pe.wait_ge(s_bank_v, j + 1)
                        tile_product(W_OUT, i, s, ring[j % 4], gH, gL, KT * kk, first=(kk == 0), last=(kk == 1),
                                     pairs=(s_gL, KT * kk, 2) if t in (0, 2) else None)
                        if kk and i:
                            mean(1, j - 2)
                else:
                    for j in range(KT):
                        pe.wait_ge(s_bank_v, KT + j + 1)
                        tile_product(BASE["p_in", 1], j // 4, j % 4, ring[j % 4], hH, hL,
                                     pairs=(s_hin, 8, 1) if j == 0 else None)
                        if j == 4:
                            pe.wait_ge(s_late, 48)
                        if j > 3 and j % 2 == 0:
                            group_product(j - 4)
                            group_product(j - 3)
                    for n in range(4, KT):
                        group_product(n)
                    for j in range(KT):
                        pe.wait_ge(s_bank_v, 2 * KT + j + 1)
                        tile_product(BASE["p_out", 1], j // 4, j % 4, ring[j % 4], gH, gL,
                                     pairs=(s_gL, SGU_FT, 2) if j == 0 else None)
                        if j > 1:
                            mean(3, j - 2)
                if layer == 0:
                    pe.wait_ge(s_keys, 32)
                n = 2 * layer + 1
                mean(n, KT - 2)
                mean(n, KT - 1)
                for t in range(17):
                    if t < 16:
                        pe.wait_ge(s_bank_a, ACT_EVACS + ACT_PER_LAYER * layer + t + 1)
                        tile_product(BASE["w_q", layer], t // 4, t % 4, ring[t % 4], hH, hL,
                                     pairs=(s_hin, 4 * n, 1) if t == 0 else None)
                    if t > 0:
                        scores(layer, t - 1)
                def grids(i, x, band):
                    pe.wait_ge(s_one, 2 * i + ((2 * layer + band) * NGRP + x + 1))
                    for t in range(GRP):
                        grid = (O, ring)[band][x][:, t * BAND:(t + 1) * BAND]
                        for part in range(3):
                            ins = mm(grid, oneB[x][:, :, t], oneA[x][:, part, :, t], start=(part == 0), stop=(part == 2))
                    ins.then_inc(s_grid, 1)

                before = ACT_EVACS + ACT_PER_LAYER * layer + 16
                stage("u", layer, s_bank_a, before, 0, 60)
                pe.wait_ge(s_sel, layer + 1)
                for a in range(3):
                    for tt in range(TT):
                        ins = nc.tensor.transpose(O[a][:, tt * P:tt * P + P], sel[:, a, tt, :], ident[:, :])
                ins.then_inc(s_selT, 1)
                stage("u", layer, s_bank_a, before, 60, BAND)
                def grid_step(i, s, band, first=False, last=False):
                    if s == 0 and not first:
                        grids(i - 1, 1, band)
                    if s == (1 if last else 2):
                        grids(i, 0, band)
                    if s == 2 and last:
                        grids(i, 1, band)

                def banded(i, **place):
                    for s in range(4):
                        pe.wait_ge(s_bank_a, 4 * i + (before + BAND + s + 1))
                        tile_product(BASE["u", layer] + BAND, i, s, ring[s], hH, hL)
                        grid_step(i, s, 0, **place)

                banded(0, first=True)
                with pe.Fori(1, PAIRS - 1) as i:
                    banded(i)
                banded(PAIRS - 1, last=True)

                base = BASE["v", layer]

                def values(i, s, first=False, last=False):
                    pe.wait_ge(s_gL2, 4 * i + (layer * EXP_TILES + s + 1))
                    for half in range(2):
                        pe.wait_ge((s_l0, s_l1)[half], 4 * i + (base + s + 1))
                        slot = (2 * s + half) % 4
                        for tt in range(TT):
                            o = O[2 * tt + half]
                            a = gateH[s % 2][:, tt * P:tt * P + P]
                            b = gateL[s % 2][:, tt * P:tt * P + P]
                            mm(o[:, :], a, wH[slot][:, :], start=first, stop=False)
                            mm(o[:, :], a, wL[slot][:, :], start=False, stop=False)
                            ins = mm(o[:, :], b, wH[slot][:, :], start=False, stop=last)
                        ins.then_inc(s_pe, 1)

                for s in range(4):
                    values(0, s, first=(s == 0))
                    if s == 1:
                        pe.wait_ge(s_bank_a, 4 + ACT_EVACS + ACT_PER_LAYER * (layer + 1))
                    grid_step(0, s, 1, first=True)
                with pe.Fori(1, PAIRS - 1) as i:
                    for s in range(4):
                        values(i, s)
                        grid_step(i, s, 1)
                for s in range(4):
                    values(PAIRS - 1, s)
                    grid_step(PAIRS - 1, s, 1, last=True)
                with pe.Fori(PAIRS, 31) as i:
                    for s in range(4):
                        values(i, s)
                for s in range(4):
                    values(31, s, last=(s == 3))
                    if layer == 0 and s == 2:
                        pe.wait_ge(s_gated, 2 * NGRP)
                        split_modulations(parts_v, 7, 2 + 7, ring[3])
                if layer == 0:
                    pe.wait_ge(s_mod, 3)
                for j in range(KT):
                    if j % 4 == 0:
                        pe.wait_ge((s_oc_a, s_oc_v)[j // 4], TT * (layer + 1))
                    for tt in range(TT):
                        ins = nc.tensor.transpose(ring[j // 2][:, (j % 2) * T + tt * P:(j % 2) * T + tt * P + P],
                                                  otok[:, tt, j * P:j * P + P], ident[:, :])
                    if j % 2:
                        ins.then_inc(s_ot, 1)
                for j in range(KT):
                    mean(2 * layer + 2, j)


def tiles_of(w, n_in):
    n = w.shape[-1]
    w = w.reshape(n_in, KT, P, n // P, P).transpose(3, 0, 2, 1, 4)
    return np.ascontiguousarray(w.reshape(n // P * n_in, P, KT * P))


def kernel(**inputs):
    import concourse.bacc as bacc
    from concourse.bass_utils import run_bass_kernel_spmd

    a = {k: np.asarray(v) for k, v in inputs.items()}

    def cols(w):
        return np.ascontiguousarray(w.reshape(-1, P).T)

    arrays = {
        "xt": np.ascontiguousarray(a["x"][0].reshape(T, KT, P).transpose(2, 1, 0)),
        "c": cols(a["c"]),
        "ada": np.ascontiguousarray(a["ada_w"].reshape(LAYERS, KT, P, CHUNKS, D).transpose(0, 3, 1, 2, 4)
                                    .reshape(LAYERS * CHUNKS * KT, P, D)),
        "adab": cols(a["ada_b"]),
        "n1": cols(a["norm1_g"]),
        "n2": cols(a["norm2_g"]),
        "fg": cols(a["final_gain"]),
        "w_in": tiles_of(a["sgu_w_in"][0], 1),
        "vg": cols(a["sgu_v_gain"]),
        "ws": np.ascontiguousarray(a["sgu_w_s"][0].transpose(2, 0, 1)),
        "bs": np.ascontiguousarray(np.broadcast_to(a["sgu_b_s"][0], (P, SGU_G, P))),
        "w_out": np.ascontiguousarray(tiles_of(a["sgu_w_out"][0], 2).reshape(KT // 2, 2, 2, P, D)
                                      .transpose(0, 2, 1, 3, 4).reshape(2 * KT, P, D)),
        "p_in": tiles_of(a["pool_w_in"][0], 1)[POOL_ORDER],
        "p_grp": np.ascontiguousarray(
            a["pool_w_grp"][0].reshape(PG, 2, P, 2, P).transpose(2, 0, 3, 1, 4).reshape(P, 8, T)),
        "ps": cols(a["pool_scale"]),
        "p_out": tiles_of(a["pool_w_out"][0].reshape(KT, P, D)[POOL_ORDER].reshape(D, D), 1),
        "w_q": np.stack([tiles_of(a["peer_w_q"][i], 1) for i in range(LAYERS)]),
        "k1": np.ascontiguousarray(a["peer_k1"].transpose(0, 3, 1, 2)),
        "k2": np.ascontiguousarray(a["peer_k2"].transpose(0, 3, 1, 2)),
        "u": np.ascontiguousarray(a["peer_u"].reshape(LAYERS, EXP_TILES, P, KT, P).transpose(0, 1, 4, 3, 2)
                                  .reshape(LAYERS, EXP_TILES, P, KT * P)),
        "v": a["peer_v"].reshape(LAYERS, EXP_TILES, P, D),
    }
    nc = bacc.Bacc("TRN2", target_bir_lowering=False, num_devices=1)
    args = [nc.dram_tensor(f"in_{k}", v.shape, mybir.dt.from_np(v.dtype), kind="ExternalInput").ap()
            for k, v in arrays.items()]
    out = nc.dram_tensor("out_t", (P, KT, T), mybir.dt.float32, kind="ExternalOutput").ap()
    build(nc, *args, out)
    r = run_bass_kernel_spmd(nc, [{f"in_{k}": v for k, v in arrays.items()}], core_ids=[0])
    return r.results[0]["out_t"].transpose(2, 1, 0).reshape(1, T, D)
```
